# Optimizing a Trainium2 kernel written in Bass

```python
import jax, jax.numpy as jnp
from jax import lax
import numpy as np

D_MODEL = 2048
BATCH = 1
SEQ = 256
DEPTH = 2

N_A = DEPTH // 2
N_B = DEPTH - N_A
CONV_WIDTH = 31
N_HEADS = 16
QK_NOPE_DIM = 128
QK_ROPE_DIM = 64
V_HEAD_DIM = 128
KV_LORA_RANK = 512
Q_LORA_RANK = 512
ROPE_THETA = 10000.0
Q_BLOCK = 128
D_FF = 4 * D_MODEL
EPS = 1e-6
NEG = -1e30

kernel_name = "yoco_conformer_mla_hybrid"

def rms_norm(x, g):
    xf = x.astype(jnp.float32)
    y = xf * lax.rsqrt(jnp.mean(xf * xf, axis=-1, keepdims=True) + EPS)
    return (y * g.astype(jnp.float32)).astype(x.dtype)

def layer_norm(x, g, b):
    xf = x.astype(jnp.float32)
    mu = jnp.mean(xf, axis=-1, keepdims=True)
    var = jnp.mean(jnp.square(xf - mu), axis=-1, keepdims=True)
    y = (xf - mu) * lax.rsqrt(var + EPS)
    return (y * g.astype(jnp.float32) + b.astype(jnp.float32)).astype(x.dtype)

def adaln(c, w, b, n):
    m = jax.nn.silu(c) @ w + b
    return jnp.split(m, n, axis=-1)

def modulate(h, shift, scale):
    return h * (1.0 + scale[:, None, :]) + shift[:, None, :]

def rope_tables(positions, dtype):
    inv = 1.0 / (ROPE_THETA ** (jnp.arange(0, QK_ROPE_DIM, 2, dtype=jnp.float32) / QK_ROPE_DIM))
    ang = positions.astype(jnp.float32)[..., None] * inv
    return jnp.cos(ang).astype(dtype), jnp.sin(ang).astype(dtype)

def apply_rope(x, cos, sin):
    x1, x2 = jnp.split(x, 2, axis=-1)
    return jnp.concatenate([x1 * cos - x2 * sin, x2 * cos + x1 * sin], axis=-1)

def conformer_conv(h, w_in, b_in, dw, dw_b, ln_g, ln_b, w_out, b_out):
    u = jax.nn.glu(h @ w_in + b_in, axis=-1)
    u = lax.conv_general_dilated(
        u, dw[:, None, :], window_strides=(1,), padding=[(CONV_WIDTH - 1, 0)],
        dimension_numbers=("NWC", "WIO", "NWC"), feature_group_count=D_MODEL) + dw_b
    u = jax.nn.silu(layer_norm(u, ln_g, ln_b))
    return u @ w_out + b_out

def mla_attention(q_nope, q_rope, k_nope, k_rope, v):
    b, s, h, _ = q_nope.shape
    nblk = s // Q_BLOCK
    scale = (QK_NOPE_DIM + QK_ROPE_DIM) ** -0.5
    qn = q_nope.reshape(b, nblk, Q_BLOCK, h, QK_NOPE_DIM).transpose(1, 0, 2, 3, 4)
    qr = q_rope.reshape(b, nblk, Q_BLOCK, h, QK_ROPE_DIM).transpose(1, 0, 2, 3, 4)
    key_pos = jnp.arange(s)

    def one_block(args):
        i, qn_b, qr_b = args
        sc = (jnp.einsum("bqhd,bkhd->bhqk", qn_b, k_nope)
              + jnp.einsum("bqhd,bkd->bhqk", qr_b, k_rope)).astype(jnp.float32) * scale
        q_pos = i * Q_BLOCK + jnp.arange(Q_BLOCK)
        mask = key_pos[None, :] <= q_pos[:, None]
        sc = jnp.where(mask[None, None], sc, NEG)
        p = jax.nn.softmax(sc, axis=-1).astype(v.dtype)
        return jnp.einsum("bhqk,bkhd->bqhd", p, v)

    out = lax.map(one_block, (jnp.arange(nblk), qn, qr))
    return out.transpose(1, 0, 2, 3, 4).reshape(b, s, h * V_HEAD_DIM)

def setup_inputs(seed: int = 0) -> dict:
    key = jax.random.key(seed)
    ks = iter(jax.random.split(key, 64))
    D = D_MODEL

    def nrm(shape, scale):
        return jax.random.normal(next(ks), shape, jnp.float32) * scale

    def gain(shape):
        return 1.0 + nrm(shape, 0.02)

    x = jax.random.normal(next(ks), (BATCH, SEQ, D), jnp.float32)
    c = jax.random.normal(next(ks), (BATCH, D), jnp.float32)
    positions = (jnp.arange(SEQ, dtype=jnp.int32)[None, :]
                 + jax.random.randint(next(ks), (BATCH, 1), 0, 1024, dtype=jnp.int32))
    ada_s = 0.1 * D ** -0.5
    return {
        "x": x, "c": c, "positions": positions,
        "w_ada_mix": nrm((DEPTH, D, 3 * D), ada_s), "b_ada_mix": nrm((DEPTH, 3 * D), 0.01),
        "w_ada_mlp": nrm((DEPTH, D, 3 * D), ada_s), "b_ada_mlp": nrm((DEPTH, 3 * D), 0.01),
        "g_pre_mix": gain((DEPTH, D)), "g_post_mix": gain((DEPTH, D)),
        "g_pre_mlp": gain((DEPTH, D)), "g_post_mlp": gain((DEPTH, D)),
        "conv_w_in": nrm((N_A, D, 2 * D), D ** -0.5), "conv_b_in": nrm((N_A, 2 * D), 0.01),
        "conv_dw": nrm((N_A, CONV_WIDTH, D), CONV_WIDTH ** -0.5), "conv_dw_b": nrm((N_A, D), 0.01),
        "conv_ln_g": gain((N_A, D)), "conv_ln_b": nrm((N_A, D), 0.01),
        "conv_w_out": nrm((N_A, D, D), D ** -0.5), "conv_b_out": nrm((N_A, D), 0.01),
        "w_ada_kv": nrm((D, 2 * D), ada_s), "b_ada_kv": nrm((2 * D,), 0.01), "g_kv": gain((D,)),
        "w_dkv": nrm((D, KV_LORA_RANK), D ** -0.5), "g_ckv": gain((KV_LORA_RANK,)),
        "w_kr": nrm((D, QK_ROPE_DIM), D ** -0.5),
        "w_uk": nrm((KV_LORA_RANK, N_HEADS * QK_NOPE_DIM), KV_LORA_RANK ** -0.5),
        "w_uv": nrm((KV_LORA_RANK, N_HEADS * V_HEAD_DIM), KV_LORA_RANK ** -0.5),
        "w_dq": nrm((N_B, D, Q_LORA_RANK), D ** -0.5), "g_cq": gain((N_B, Q_LORA_RANK)),
        "w_uq": nrm((N_B, Q_LORA_RANK, N_HEADS * (QK_NOPE_DIM + QK_ROPE_DIM)), Q_LORA_RANK ** -0.5),
        "w_o": nrm((N_B, N_HEADS * V_HEAD_DIM, D), (N_HEADS * V_HEAD_DIM) ** -0.5),
        "mlp_w_up": nrm((DEPTH, D, D_FF), D ** -0.5),
        "mlp_w_down": nrm((DEPTH, D_FF, D), D_FF ** -0.5),
    }

def reference(x, c, positions,
              w_ada_mix, b_ada_mix, w_ada_mlp, b_ada_mlp,
              g_pre_mix, g_post_mix, g_pre_mlp, g_post_mlp,
              conv_w_in, conv_b_in, conv_dw, conv_dw_b, conv_ln_g, conv_ln_b, conv_w_out, conv_b_out,
              w_ada_kv, b_ada_kv, g_kv,
              w_dkv, g_ckv, w_kr, w_uk, w_uv,
              w_dq, g_cq, w_uq, w_o,
              mlp_w_up, mlp_w_down):
    b, s, _ = x.shape
    cos, sin = rope_tables(positions, x.dtype)
    h = x
    k_nope = k_rope = v = None
    for l in range(DEPTH):
        shift, scale, gate = adaln(c, w_ada_mix[l], b_ada_mix[l], 3)
        hn = modulate(rms_norm(h, g_pre_mix[l]), shift, scale)
        if l < N_A:
            y = conformer_conv(hn, conv_w_in[l], conv_b_in[l], conv_dw[l], conv_dw_b[l],
                               conv_ln_g[l], conv_ln_b[l], conv_w_out[l], conv_b_out[l])
        else:
            j = l - N_A
            if j == 0:
                kv_shift, kv_scale = adaln(c, w_ada_kv, b_ada_kv, 2)
                kvn = modulate(rms_norm(h, g_kv), kv_shift, kv_scale)
                c_kv = rms_norm(kvn @ w_dkv, g_ckv)
                k_nope = (c_kv @ w_uk).reshape(b, s, N_HEADS, QK_NOPE_DIM)
                v = (c_kv @ w_uv).reshape(b, s, N_HEADS, V_HEAD_DIM)
                k_rope = apply_rope(kvn @ w_kr, cos, sin)
            c_q = rms_norm(hn @ w_dq[j], g_cq[j])
            q = (c_q @ w_uq[j]).reshape(b, s, N_HEADS, QK_NOPE_DIM + QK_ROPE_DIM)
            q_nope = q[..., :QK_NOPE_DIM]
            q_rope = apply_rope(q[..., QK_NOPE_DIM:], cos[:, :, None, :], sin[:, :, None, :])
            y = mla_attention(q_nope, q_rope, k_nope, k_rope, v) @ w_o[j]
        h = h + gate[:, None, :] * rms_norm(y, g_post_mix[l])
        shift, scale, gate = adaln(c, w_ada_mlp[l], b_ada_mlp[l], 3)
        hn = modulate(rms_norm(h, g_pre_mlp[l]), shift, scale)
        y = jnp.square(jax.nn.relu(hn @ mlp_w_up[l])) @ mlp_w_down[l]
        h = h + gate[:, None, :] * rms_norm(y, g_post_mlp[l])
    return h


_drawn_inputs = setup_inputs


def setup_inputs(seed=0):
    import zlib

    import numpy as np

    out = dict(_drawn_inputs(seed))
    spreads = {}
    factors = {'b_ada_mix': 3.95,
     'b_ada_mlp': 4.01,
     'g_pre_mix': 8.0,
     'g_post_mix': 8.0,
     'g_pre_mlp': 8.0,
     'g_post_mlp': 8.0,
     'conv_b_in': 8.0,
     'conv_dw_b': 8.0,
     'conv_ln_g': 8.0,
     'conv_ln_b': 8.0,
     'conv_b_out': 8.0,
     'b_ada_kv': 8.0,
     'g_kv': 8.0,
     'g_ckv': 8.0,
     'g_cq': 8.0}
    for name, (base, spread) in spreads.items():
        noise = np.random.default_rng([zlib.crc32(name.encode()), seed]).standard_normal(out[name].shape)
        drawn = base * np.exp(spread * noise) if base else spread * noise
        out[name] = __import__('jax').numpy.asarray(drawn.astype(out[name].dtype))
    for name, factor in factors.items():
        out[name] = (out[name] * factor).astype(out[name].dtype)
    return out
```

```python
from collections import namedtuple
from contextlib import ExitStack

import concourse.bass as bass
import numpy as np
from concourse import mybir

P = 128
D = 2048
T = 256
NT = D // P
WIDTH = 31
HEADS, NOPE, ROPE, VDIM, RANK = 16, 128, 64, 128, 512
RT = RANK // P
FF = 4 * D
CHUNKS = FF // D
THETA = 10000.0
EPS = 1e-6
SCALE = float(NOPE + ROPE) ** -0.5
NEG = -1e30
PIECE = 2048
GT = 4
GP = NT // 4

G_IN, G_OUT, G_MLP0 = 0, 8, 12
G_KR = G_MLP0 + 2 * GT * CHUNKS
G_DKV, G_DQ, G_WO = G_KR + 1, G_KR + 2, G_KR + 3
G_MLP1 = G_WO + 4
N_IN, N_OUT, N_MLP0 = 0, 32, 48
N_KR = N_MLP0 + 8 * GP * CHUNKS
N_DKV, N_DQ = N_KR + 1, N_KR + 1 + GP
N_PAIR = N_DQ + GP
N_WO = N_PAIR + HEADS
N_MLP1 = N_WO + 4 * GP
N_ALL = N_MLP1 + 8 * GP * CHUNKS

M_MIX0, M_MLP0, M_KV, M_MIX1, M_MLP1 = 0, 48, 96, 128, 176
M_ALL = 224
A_START, A_CONV, A_MLP0 = 32, 4, 3
A_IN, A_OUT, A_M0 = 32, 64, 80
A_ATT = A_M0 + 2 * GT * CHUNKS * A_MLP0
A_PAIR = A_ATT + 8
A_WO = A_PAIR + 16

C_BADA = 0
C_PREMIX, C_POSTMIX, C_PREMLP, C_POSTMLP = 224, 256, 288, 320
C_BIN = 352
C_DW = 384
C_LNG = C_DW + NT * (WIDTH + 1)
C_LNB, C_BOUT, C_GKV = C_LNG + 16, C_LNG + 32, C_LNG + 48
C_GCKV, C_GCQ = C_LNG + 64, C_LNG + 68
C_ALL = C_LNG + 72
K_INV, K_SIGN, K_IDENT, K_MASK = 0, 1, 2, 130
K_ALL = K_MASK + 3 * P

S_H0, S_MU, S_VAR, S_Y0, S_H1, S_Y1, S_H2, S_CKV, S_CQ, S_Y2, S_H3, S_Y3 = range(12)
QUARTERS = [4, 4, 4, 4, 4, 4, 4, 1, 1, 4, 4, 4]

Pos = namedtuple("Pos", "static step loop")


def fixed(n):
    return Pos(n, 0, None)


def ahead(p, k):
    return Pos(p.static + k, p.step, p.loop)


def value(p, plus=0, times=1):
    n = times * (p.static + plus)
    return n if p.loop is None else n + times * p.step * p.loop


def turn(p, ring):
    n = p.static // ring
    return Pos(n, p.step // ring, p.loop)


def wait(eng, sem, v):
    if not (isinstance(v, int) and v <= 0):
        eng.wait_ge(sem, v)


def trunk(nc, x_t, c, pos, cols_d, consts_d, w_stream, ada_stream, out_t):
    f32, f32r, i32 = mybir.dt.float32, mybir.dt.float32r, mybir.dt.int32
    ALU, ACT, AX = mybir.AluOpType, mybir.ActivationFunctionType, mybir.AxisListType
    ctx = ExitStack()
    with ctx:
        def sb(name, shape, dt=f32):
            return ctx.enter_context(nc.sbuf_tensor(name, shape, dt))

        def sem(name):
            return ctx.enter_context(nc.semaphore(name))

        h = sb("h", [P, NT, T])
        xn = sb("xn", [P, NT, 2, T], f32r)
        hid = sb("hid", [P, NT, 2, T], f32r)
        y = sb("y", [P, NT, T])
        raw = sb("raw", [P, 4, PIECE])
        wsp = sb("wsp", [P, 2, 2, PIECE], f32r)
        ada = sb("ada", [P, 2, PIECE])
        cb = sb("cb", [P, D])
        s0 = sb("s0", [P, 4, T])
        s1 = sb("s1", [P, 4, T])
        s2 = sb("s2", [P, 4, T])
        root = sb("root", [P, T])
        rstd = sb("rstd", [P, T])
        mod = sb("mod", [P, M_ALL])
        mod_step = sb("mod_step", [P, 8])
        cols = sb("cols", [P, C_ALL])
        consts = sb("consts", [P, K_ALL])
        co_a = sb("co_a", [P, NT])
        co_b = sb("co_b", [P, NT])
        co_a2 = sb("co_a2", [P, NT])
        co_b2 = sb("co_b2", [P, NT])
        co_g = sb("co_g", [P, NT])
        epsc = sb("epsc", [P, 2])
        ones = sb("ones", [P, P])
        posi = sb("posi", [P, T], i32)
        table = sb("table", [P, T])
        krope = sb("krope", [ROPE, T])
        ubuf = sb("ubuf", [P, 2, WIDTH - 1 + T])
        dwg = sb("dwg", [P, 2, WIDTH + 1])
        stat = sb("stat", [P, 3, 2, 2])
        ps = ctx.enter_context(nc.psum_tensor("ps", [P, 8, 512], f32))

        yw = y[:, :, :].rearrange("p t n -> p (t n)")
        qn = yw[:, 0:512].rearrange("p (j n) -> p j n", j=2)
        qr = yw[0:ROPE, 512:1024].rearrange("p (j n) -> p j n", j=2)
        kn = yw[:, 1024:1536].rearrange("p (j n) -> p j n", j=2)
        vv = yw[:, 1536:2560].rearrange("p (b k n) -> p b k n", b=2, k=2)
        pr = yw[:, 2560:3328].rearrange("p (j n) -> p j n", j=2)
        prt = yw[:, 3328:4096].rearrange("p (j n) -> p j n", j=2)
        ident = consts[:, K_IDENT:K_IDENT + P]
        mask = consts[:, K_MASK:K_MASK + 3 * P].rearrange("p (o n) -> p o n", o=1)

        small_loaded, c_loaded = sem("small_loaded"), sem("c_loaded")
        h_loaded = [sem(f"h_loaded{q}") for q in range(4)]
        w_loaded = [sem(f"w_loaded{s}") for s in range(4)]
        ada_loaded = [sem(f"ada_loaded{s}") for s in range(2)]
        ada_used = sem("ada_used")
        c_ready = sem("c_ready")
        hi_ready = sem("hi_ready")
        lo_ready = sem("lo_ready")
        split_used = sem("split_used")
        low_copied = sem("low_copied")
        summed = sem("summed")
        evac_done = sem("evac_done")
        hid_hi = sem("hid_hi")
        hid_ready = sem("hid_ready")
        biased = sem("biased")
        sig_ready = sem("sig_ready")
        u_ready = sem("u_ready")
        taps = sem("taps")
        squares = sem("squares")
        partial = sem("partial")
        total = sem("total")
        root_ready = sem("root_ready")
        rstd_ready = sem("rstd_ready")
        centred = sem("centred")
        scaled = sem("scaled")
        silu_done = sem("silu_done")
        h_ready = sem("h_ready")
        xf_ready = sem("xf_ready")
        xhi = sem("xhi")
        x_ready = sem("x_ready")
        step_done = sem("step_done")
        trig = sem("trig")
        ang = sem("ang")
        kv_copied = sem("kv_copied")
        q_ready = sem("q_ready")
        q_step = sem("q_step")
        scores = sem("scores")
        masked = sem("masked")
        maxed = sem("maxed")
        exps = sem("exps")
        prob_step = sem("prob_step")
        turned = sem("turned")
        prt_ready = sem("prt_ready")
        o_done = sem("o_done")
        o_hi = sem("o_hi")
        o_ready = sem("o_ready")
        stored = sem("stored")

        def stat_bank(k):
            return 4 * (G_DKV % 2) if k == S_CKV else 0

        sbase = [sum(QUARTERS[:k]) for k in range(len(QUARTERS) + 1)]

        def group_order(pieces, adas):
            out, a = [], 0
            for k in range(pieces):
                out.append(("w", k + 2))
                while a * pieces < adas * (k + 1):
                    out.append(("a", a))
                    a += 1
            return out

        def run_order(order, p, a, do_w, do_a):
            for kind, k in order:
                if kind == "w":
                    if p.loop is not None or p.static + k < N_ALL:
                        do_w(ahead(p, k))
                else:
                    do_a(ahead(a, k))

        def looped(eng, count, body):
            body(None)
            with eng.Fori(1, count) as i:
                body(i)

        def mlp(eng, group, g0, n0, a0, per, u0, last):
            def two(kind, c, i, off, final=False):
                loop = i if c is None else (4 * c + i if i is not None else 4 * c)
                for j in range(2):
                    k = off + j
                    group(kind, Pos(g0 + k, 2, loop), Pos(n0 + GP * k, 2 * GP, loop),
                          Pos(a0 + per * k, 2 * per, loop), per,
                          Pos(j, 2, i), chunk_u(c), j)

            def chunk_u(c):
                return Pos(u0, 4, c) if c is not None else None

            def chunk(c):
                with eng.Fori(0, 2) as i:
                    two("up", c, i, 0)
                with eng.Fori(0, 2) as i:
                    two("down", c, i, 4)

            with eng.Fori(0, CHUNKS - last) as c:
                chunk(c)
            if last:
                k = 8 * (CHUNKS - 1)
                g, n, u = g0 + k, n0 + GP * k, Pos(u0 + 4 * (CHUNKS - 1), 0, None)
                with eng.Fori(0, 2) as i:
                    for j in range(2):
                        group("up", Pos(g + j, 2, i), Pos(n + GP * j, 2 * GP, i), fixed(0), 0, Pos(j, 2, i), u, j)
                for k in range(4):
                    group("down", fixed(g + 4 + k), fixed(n + GP * (4 + k)), fixed(0), 0, fixed(k), u, k % 2)

        block = ctx.enter_context(nc.Block())

        @block.sync
        def _(sp):
            def load_w(p):
                s = p.static % 4
                wait(sp, lo_ready, value(p, -3))
                sp.dma_start(raw[:, s, :], w_stream[value(p)]).then_inc(w_loaded[s], 16)

            def load_a(a):
                s = a.static % 2
                wait(sp, ada_used, value(a, -1))
                sp.dma_start(ada[:, s, :], ada_stream[value(a)]).then_inc(ada_loaded[s], 16)

            sp.dma_start(cb[:, :], c.rearrange("(o n) -> o n", o=1).broadcast_to([P, D])).then_inc(c_loaded, 16)
            load_a(fixed(0))
            load_a(fixed(1))
            for q in range(4):
                sp.dma_start(h[:, 4 * q:4 * q + 4, :], x_t[:, 4 * q:4 * q + 4, :]).then_inc(h_loaded[q], 16)
            sp.dma_start(cols[:, :], cols_d).then_inc(small_loaded, 16)
            sp.dma_start(consts[:, :], consts_d).then_inc(small_loaded, 16)
            sp.dma_start(posi[:, :], pos.rearrange("(o n) -> o n", o=1).broadcast_to([P, T])).then_inc(small_loaded, 16)
            for a in range(2, A_START):
                load_a(fixed(a))
            load_w(fixed(0))
            load_w(fixed(1))

            def group(kind, g, n, a, per, t, u, j):
                run_order(group_order(GP, per), n, a, load_w, load_a)

            def conv_groups(g0, n0, a0, count):
                def body(i):
                    for j in range(2):
                        group("", None, Pos(n0 + GP * j, 2 * GP, i), Pos(a0 + A_CONV * j, 2 * A_CONV, i), A_CONV, None, None, j)
                looped(sp, count // 2, body)

            conv_groups(G_IN, N_IN, A_IN, 8)
            conv_groups(G_OUT, N_OUT, A_OUT, 4)
            mlp(sp, group, G_MLP0, N_MLP0, A_M0, A_MLP0, 0, 0)
            run_order(group_order(1, 0), fixed(N_KR), fixed(0), load_w, load_a)
            run_order(group_order(GP, 4), fixed(N_DKV), fixed(A_ATT), load_w, load_a)
            run_order(group_order(GP, 4), fixed(N_DQ), fixed(A_ATT + 4), load_w, load_a)

            def pairs(i, off):
                for k in range(2):
                    run_order(group_order(2, 2), Pos(N_PAIR + 4 * off + 2 * k, 4, i), Pos(A_PAIR + 4 * off + 2 * k, 4, i), load_w, load_a)
            looped(sp, 3, lambda i: pairs(i, 0))
            pairs(None, 3)

            def wo(i):
                for k in range(2):
                    run_order(group_order(GP, 6), Pos(N_WO + GP * k, 2 * GP, i), Pos(A_WO + 6 * k, 12, i), load_w, load_a)
            looped(sp, 2, wo)
            mlp(sp, group, G_MLP1, N_MLP1, 0, 0, 16, 1)
            for q in range(4):
                sp.wait_ge(h_ready, 12 + q + 1)
                sp.dma_start(out_t[:, 4 * q:4 * q + 4, :], h[:, 4 * q:4 * q + 4, :]).then_inc(stored, 16)
            sp.wait_ge(stored, 64)

        @block.scalar
        def _(act):
            def split_hi(p):
                s, d = p.static % 4, p.static % 2
                wait(act, w_loaded[s], value(turn(p, 4), 1, 16))
                wait(act, split_used, value(p, -1))
                act.activation(wsp[:, d, 0, :], raw[:, s, :], ACT.Copy).then_inc(hi_ready, 1)

            def halves(g, n, b, tiles=4, pieces=GP):
                act.wait_ge(split_used, value(n, pieces))
                wait(act, summed, value(g))
                act.activation(s1[:, 0:tiles, :], ps[:, b:b + tiles, T:2 * T], ACT.Copy).then_inc(low_copied, 1)

            def group(kind, g, n, a, per, t, u, j):
                run_order(group_order(GP, 0), n, a, split_hi, None)
                halves(g, n, 4 * (g.static % 2))
                if kind == "up":
                    act.wait_ge(evac_done, value(g, 1))
                    act.activation(hid[:, bass.ds(value(t, 0, 4), 4), 0, :], s2[:, :, :], ACT.Copy).then_inc(hid_hi, 1)

            def square(k, q, src, ready, at):
                b = sbase[k] + q
                act.wait_ge(ready, at)
                wait(act, partial, b - 1)
                act.activation((s0, s1)[b % 2][:, :, :], src, ACT.Square).then_inc(squares, 1)

            def take_root(k, n):
                act.wait_ge(total, k + 1)
                wait(act, rstd_ready, k - (k > S_MU))
                act.activation(root[:, :], ps[:, stat_bank(k), 0:T], ACT.Sqrt, bias=epsc[:, 0:1], scale=1.0 / n).then_inc(root_ready, 1)

            def high(dst, q, i):
                act.wait_ge(xf_ready, i + 1)
                act.activation(dst[:, 4 * q:4 * q + 4, 0, :], y[:, 4 * q:4 * q + 4, :], ACT.Copy).then_inc(xhi, 1)

            def quarter(buf, q):
                return buf[:, 4 * q:4 * q + 4, :]

            act.wait_ge(c_loaded, 16)
            act.activation(cb[:, :], cb[:, :], ACT.Silu).then_inc(c_ready, 1)
            act.wait_ge(ang, 1)
            act.activation(table[64:128, :], rstd[64:128, :], ACT.Sin, scale=consts[64:128, K_SIGN:K_SIGN + 1]).then_inc(trig, 1)
            act.wait_ge(ang, 2)
            act.activation(table[0:64, :], root[0:64, :], ACT.Sin, scale=-1.0, bias=epsc[0:64, 1:2]).then_inc(trig, 1)
            for q in range(4):
                square(S_H0, q, quarter(h, q), h_loaded[q], 16)
            take_root(S_H0, D)
            split_hi(fixed(0))
            split_hi(fixed(1))
            for q in range(4):
                high(xn, q, q)

            def conv_in(i):
                for j in range(2):
                    g, n = Pos(G_IN + j, 2, i), Pos(N_IN + GP * j, 2 * GP, i)
                    run_order(group_order(GP, 0), n, None, split_hi, None)
                    halves(g, n, 4 * j)
                    act.wait_ge(biased, value(g, 1))
                    act.activation(s2[:, 0:2, :], s0[:, 2:4, :], ACT.Sigmoid).then_inc(sig_ready, 1)
            looped(act, 4, conv_in)

            act.wait_ge(total, S_MU + 1)
            act.wait_ge(rstd_ready, S_MU)
            act.activation(root[:, :], ps[:, 0, 0:T], ACT.Copy, scale=1.0 / D).then_inc(root_ready, 1)
            for q in range(4):
                square(S_VAR, q, quarter(y, q), centred, q + 1)
            take_root(S_VAR, D)
            for q in range(4):
                act.wait_ge(scaled, q + 1)
                for t in range(4 * q, 4 * q + 4):
                    last = act.activation(y[:, t, :], y[:, t, :], ACT.Silu, bias=cols[:, C_LNB + t:C_LNB + t + 1],
                                          scale=cols[:, C_LNG + t:C_LNG + t + 1])
                last.then_inc(silu_done, 1)
                act.wait_ge(silu_done, q + 1)
                act.activation(hid[:, 4 * q:4 * q + 4, 0, :], quarter(y, q), ACT.Copy).then_inc(xhi, 1)

            def conv_out(i):
                for j in range(2):
                    group("out", Pos(G_OUT + j, 2, i), Pos(N_OUT + GP * j, 2 * GP, i), None, 0, None, None, j)
            looped(act, 2, conv_out)

            def post_and_pre(ky, kh, r, outs):
                for q in range(4):
                    square(ky, q, quarter(y, q), evac_done, {S_Y0: G_MLP0, S_Y1: G_KR, S_Y2: G_MLP1, S_Y3: G_MLP1 + 8 * CHUNKS}[ky])
                take_root(ky, D)
                if kh is None:
                    return
                for q in range(4):
                    square(kh, q, quarter(h, q), h_ready, 4 * r + q + 1)
                take_root(kh, D)
                for dst, i in outs:
                    for q in range(4):
                        high(dst, q, i + q)

            post_and_pre(S_Y0, S_H1, 0, [(xn, 4)])
            mlp(act, group, G_MLP0, N_MLP0, 0, 0, 0, 0)
            post_and_pre(S_Y1, S_H2, 1, [(xn, 8), (hid, 12)])

            split_hi(fixed(N_KR + 2))
            halves(fixed(G_KR), fixed(N_KR), 4 * (G_KR % 2), 1, 1)
            run_order(group_order(GP, 0), fixed(N_DKV), None, split_hi, None)
            halves(fixed(G_DKV), fixed(N_DKV), 4 * (G_DKV % 2))

            def rank_norm(k, i, at):
                square(k, 0, quarter(y, i), evac_done, at)
                take_root(k, RANK)
                act.wait_ge(xf_ready, 16 + i + 1)
                act.activation(xn[:, 4 * i:4 * i + 4, 0, :], quarter(y, i), ACT.Copy).then_inc(xhi, 1)

            rank_norm(S_CKV, 0, G_DKV + 1)
            run_order(group_order(GP, 0), fixed(N_DQ), None, split_hi, None)
            halves(fixed(G_DQ), fixed(N_DQ), 4 * (G_DQ % 2))
            rank_norm(S_CQ, 1, G_DQ + 1)

            def evac_proj(p):
                b = p.static % 2
                act.wait_ge(split_used, value(p, 1, 2) + N_PAIR)
                act.wait_ge(x_ready, 22)
                wait(act, scores, value(p))
                act.activation(kn, ps[:, 0, :].rearrange("p (j n) -> p j n", j=2), ACT.Copy)
                wait(act, o_done, value(p, -1))
                act.activation(vv[:, b], ps[:, 1, :].rearrange("p (j n) -> p j n", j=2), ACT.Copy).then_inc(kv_copied, 1)

            def pair(p, n, more):
                for k in range(2):
                    split_hi(ahead(n, 2 + k))
                act.wait_ge(maxed, value(p, 1, 2))
                for j in range(2):
                    for t in range(2):
                        lo, hi = (0, P) if t == 0 else (P, 3 * P)
                        last = act.activation(pr[:, j, lo:hi], pr[:, j, lo:hi], ACT.Exp, bias=stat[:, 0, j, t:t + 1],
                                              scale=SCALE, accum_out=stat[:, 1, j, t:t + 1])
                last.then_inc(exps, 1)
                if more:
                    evac_proj(ahead(p, 1))
                act.wait_ge(turned, value(p, 1))
                wait(act, o_done, value(p))
                act.activation(prt, ps[:, 6:8, 0:3 * P], ACT.Copy).then_inc(prt_ready, 1)
                act.wait_ge(o_done, value(p, 1))
                act.activation(hid[:, bass.ds(value(p, 0, 2), 2), 0, :], ps[:, 4, :].rearrange("p (j n) -> p j n", j=2), ACT.Copy).then_inc(o_hi, 1)

            evac_proj(fixed(0))
            looped(act, 3, lambda i: [pair(Pos(k, 2, i), Pos(N_PAIR + 2 * k, 4, i), True) for k in range(2)])
            pair(fixed(6), fixed(N_PAIR + 12), True)
            pair(fixed(7), fixed(N_PAIR + 14), False)

            def wo(i):
                for j in range(2):
                    n = Pos(N_WO + GP * j, 2 * GP, i)
                    run_order(group_order(GP, 0), n, None, split_hi, None)
                    halves(Pos(G_WO + j, 2, i), n, 4 * ((G_WO + j) % 2))
            looped(act, 2, wo)
            post_and_pre(S_Y2, S_H3, 2, [(xn, 18)])
            mlp(act, group, G_MLP1, N_MLP1, 0, 0, 16, 1)
            post_and_pre(S_Y3, None, 3, [])

        @block.vector
        def _(ve):
            steps = [0]

            def step(ins):
                steps[0] += 1
                ins.then_inc(step_done, 1)

            def settled():
                ve.wait_ge(step_done, steps[0])

            def split_lo(p):
                s, d = p.static % 4, p.static % 2
                ve.wait_ge(hi_ready, value(p, 1))
                ve.tensor_tensor(wsp[:, d, 1, :], raw[:, s, :], wsp[:, d, 0, :].bitcast(f32), ALU.subtract).then_inc(lo_ready, 1)

            def mod_column(a):
                if a.loop is None:
                    return mod[:, a.static:a.static + 1]
                return mod_step[:, a.static % 8:a.static % 8 + 1]

            def keep_mod(a, per):
                if a.loop is not None and per:
                    ve.wait_ge(ada_used, value(a, per))
                    for k in range(per):
                        c0 = (a.static + k) % 8
                        ve.tensor_copy(mod[:, bass.ds(value(a, k), 1)], mod_step[:, c0:c0 + 1])

            def reduce_ada(a):
                s = a.static % 2
                ve.wait_ge(ada_loaded[s], value(turn(a, 2), 1, 16))
                ve.tensor_tensor_reduce(out=ada[:, s, :], in0=ada[:, s, :], in1=cb[:, :], scale=1.0, scalar=0.0,
                                        op0=ALU.mult, op1=ALU.add, accum_out=mod_column(a)).then_inc(ada_used, 1)

            def add_halves(g, b):
                ve.wait_ge(low_copied, value(g, 1))
                wait(ve, evac_done, value(g))
                ve.tensor_tensor(s0[:, :, :], ps[:, b:b + 4, 0:T], s1[:, :, :], ALU.add).then_inc(summed, 1)
                ve.wait_ge(summed, value(g, 1))

            def group(kind, g, n, a, per, t, u, j):
                run_order(group_order(GP, per), n, a, split_lo, reduce_ada)
                keep_mod(a, per)
                add_halves(g, 4 * (g.static % 2))
                at = bass.ds(value(t, 0, 4), 4)
                if kind == "down":
                    ve.tensor_tensor(y[:, at, :], y[:, at, :], s0[:, :, :], ALU.add).then_inc(evac_done, 1)
                    return
                done = value(u, t.static) + (2 * t.loop if t.loop is not None else 0)
                ve.scalar_tensor_tensor(s2[:, :, :], s0[:, :, :], 0.0, s0[:, :, :], ALU.max, ALU.mult).then_inc(evac_done, 1)
                ve.wait_ge(hid_hi, done + 1)
                ve.tensor_tensor(hid[:, at, 1, :], s2[:, :, :], hid[:, at, 0, :].bitcast(f32), ALU.subtract).then_inc(hid_ready, 1)
                ve.wait_ge(hid_ready, done + 1)

            def quarter(buf, q):
                return buf[:, 4 * q:4 * q + 4, :]

            def wide(v, n=4):
                return v.rearrange("p (o n) -> p o n", o=1).broadcast_to([P, n, T])

            def over_tiles(k, q, src):
                wait(ve, total, k)
                ve.tensor_reduce(s2[:, q, :], src.rearrange("p t n -> p n t"), AX.X, ALU.add).then_inc(partial, 1)

            def sum_squares(k):
                for q in range(QUARTERS[k]):
                    b = sbase[k] + q
                    ve.wait_ge(squares, b + 1 - 4 * (k > S_MU))
                    over_tiles(k, q, (s0, s1)[(b - 0) % 2][:, :, :])

            def deviation(k):
                ve.wait_ge(root_ready, k + 1)
                ve.reciprocal(rstd[:, :], root[:, :]).then_inc(rstd_ready, 1)
                ve.wait_ge(rstd_ready, k + (k < S_MU))

            def scale_shift(ca, cb_, m, gain):
                step(ve.tensor_tensor(cb_[:, :], mod[:, m:m + NT], cols[:, C_BADA + m:C_BADA + m + NT], ALU.add))
                step(ve.tensor_tensor(ca[:, :], mod[:, m + NT:m + 2 * NT], cols[:, C_BADA + m + NT:C_BADA + m + 2 * NT], ALU.add))
                settled()
                step(ve.scalar_tensor_tensor(ca[:, :], ca[:, :], 1.0, cols[:, gain:gain + NT], ALU.add, ALU.mult))
                settled()

            def gate_gain(m, gain):
                step(ve.tensor_tensor(co_g[:, :], mod[:, m:m + NT], cols[:, C_BADA + m:C_BADA + m + NT], ALU.add))
                settled()
                step(ve.tensor_tensor(co_g[:, :], co_g[:, :], cols[:, gain:gain + NT], ALU.mult))
                settled()

            def modulated(dst, ca, cb_, i):
                def times(q):
                    step(ve.tensor_tensor(quarter(y, q), quarter(h, q), wide(rstd[:, :]), ALU.mult))
                times(0)
                for q in range(4):
                    settled()
                    for t in range(4 * q, 4 * q + 4):
                        last = ve.tensor_scalar(y[:, t, :], y[:, t, :], ca[:, t:t + 1], cb_[:, t:t + 1], ALU.mult, ALU.add)
                    last.then_inc(xf_ready, 1)
                    if q < 3:
                        times(q + 1)
                    ve.wait_ge(xhi, i + q + 1)
                    ve.tensor_tensor(dst[:, 4 * q:4 * q + 4, 1, :], quarter(y, q), dst[:, 4 * q:4 * q + 4, 0, :].bitcast(f32),
                                     ALU.subtract).then_inc(x_ready, 1)

            def residual(k, m, gain):
                sum_squares(k)
                gate_gain(m, gain)
                deviation(k)

                def times(q):
                    step(ve.tensor_tensor(quarter(y, q), quarter(y, q), wide(rstd[:, :]), ALU.mult))
                times(0)
                for q in range(4):
                    at = steps[0]
                    if q < 3:
                        times(q + 1)
                    ve.wait_ge(step_done, at)
                    for t in range(4 * q, 4 * q + 4):
                        last = ve.scalar_tensor_tensor(h[:, t, :], y[:, t, :], co_g[:, t:t + 1], h[:, t, :], ALU.mult, ALU.add)
                    last.then_inc(h_ready, 1)

            ve.memset(epsc[:, 0:1], EPS)
            ve.memset(epsc[:, 1:2], float(np.pi / 2))
            ve.memset(ones[:, :], 1.0)
            step(ve.memset(ubuf[:, :, :], 0.0))
            ve.wait_ge(small_loaded, 48)
            step(ve.tensor_copy(rstd[:, :], posi[:, :]))
            settled()
            step(ve.tensor_scalar(rstd[:, :], rstd[:, :], consts[:, K_INV:K_INV + 1], None, ALU.mult))
            settled()
            magic = 1.5 * 2.0 ** 23
            step(ve.tensor_scalar(root[:, :], rstd[:, :], float(1 / (2 * np.pi)), magic, ALU.mult, ALU.add))
            settled()
            step(ve.tensor_scalar(root[:, :], root[:, :], magic, None, ALU.subtract))
            settled()
            part1 = 6.28125
            part2 = float(np.float32(np.round((2 * np.pi - part1) * 2 ** 22) / 2 ** 22))
            part3 = float(2 * np.pi - part1 - part2)
            for part in (part1, part2, part3):
                step(ve.scalar_tensor_tensor(rstd[:, :], root[:, :], -part, rstd[:, :], ALU.mult, ALU.add))
                settled()
            below = float(np.nextafter(np.float32(np.pi), np.float32(0)))
            ve.tensor_scalar(rstd[:, :], rstd[:, :], below, -below, ALU.min, ALU.max).then_inc(ang, 1)
            ve.wait_ge(ang, 1)
            ve.scalar_tensor_tensor(root[:, :], rstd[:, :], -1.0, rstd[:, :], ALU.mult, ALU.max).then_inc(ang, 1)

            ve.wait_ge(c_ready, 1)
            for a in range(A_START):
                reduce_ada(fixed(a))
            ve.wait_ge(trig, 2)
            sum_squares(S_H0)
            split_lo(fixed(0))
            split_lo(fixed(1))
            ve.wait_ge(ada_used, A_START)
            scale_shift(co_a, co_b, M_MIX0, C_PREMIX)
            deviation(S_H0)
            modulated(xn, co_a, co_b, 0)

            def conv_in(i):
                for j in range(2):
                    g, n = Pos(G_IN + j, 2, i), Pos(N_IN + GP * j, 2 * GP, i)
                    a = Pos(A_IN + A_CONV * j, 2 * A_CONV, i)
                    run_order(group_order(GP, A_CONV), n, a, split_lo, reduce_ada)
                    keep_mod(a, A_CONV)
                    add_halves(g, 4 * j)
                    bias = cols[:, bass.ds(value(g, 0, 4) + C_BIN, 4)].rearrange("p (t o) -> p t o", o=1).broadcast_to([P, 4, T])
                    ve.tensor_tensor(s0[:, :, :], s0[:, :, :], bias, ALU.add).then_inc(biased, 1)
                    ve.tensor_copy(dwg[:, :, :].rearrange("p j w -> p (j w)"),
                                   cols[:, bass.ds(value(g, 0, 2 * (WIDTH + 1)) + C_DW, 2 * (WIDTH + 1))])
                    ve.wait_ge(sig_ready, value(g, 1))
                    ve.tensor_tensor(ubuf[:, :, WIDTH - 1:], s0[:, 0:2, :], s2[:, 0:2, :], ALU.mult).then_inc(u_ready, 1)
                    ve.wait_ge(u_ready, value(g, 1))
                    for w in range(WIDTH):
                        for t in range(2):
                            acc, u = s2[:, 2 + t, :], ubuf[:, t, w:w + T]
                            if w == 0:
                                ve.tensor_scalar(acc, u, dwg[:, t, 0:1], dwg[:, t, WIDTH:WIDTH + 1], ALU.mult, ALU.add).then_inc(taps, 1)
                                continue
                            ve.wait_ge(taps, value(g, 0, 2 * WIDTH - 1) + 2 * (w - 1) + t + 1)
                            out = y[:, bass.ds(value(g, 0, 2) + t, 1), :].rearrange("p o n -> p (o n)") if w == WIDTH - 1 else acc
                            final = w == WIDTH - 1 and t == 1
                            ve.scalar_tensor_tensor(out, u, dwg[:, t, w:w + 1], acc, ALU.mult, ALU.add).then_inc(evac_done if final else taps, 1)
            looped(ve, 4, conv_in)

            ve.wait_ge(evac_done, G_OUT)
            for q in range(4):
                over_tiles(S_MU, q, quarter(y, q))
            ve.wait_ge(root_ready, S_MU + 1)
            for q in range(4):
                ve.tensor_tensor(quarter(y, q), quarter(y, q), wide(root[:, :]), ALU.subtract).then_inc(centred, 1)
            sum_squares(S_VAR)
            deviation(S_VAR)
            for q in range(4):
                ve.tensor_tensor(quarter(y, q), quarter(y, q), wide(rstd[:, :]), ALU.mult).then_inc(scaled, 1)
            for q in range(4):
                ve.wait_ge(xhi, 4 + q + 1)
                ve.tensor_tensor(hid[:, 4 * q:4 * q + 4, 1, :], quarter(y, q), hid[:, 4 * q:4 * q + 4, 0, :].bitcast(f32),
                                 ALU.subtract).then_inc(x_ready, 1)

            def conv_out(i):
                for j in range(2):
                    g, n = Pos(G_OUT + j, 2, i), Pos(N_OUT + GP * j, 2 * GP, i)
                    a = Pos(A_OUT + A_CONV * j, 2 * A_CONV, i)
                    run_order(group_order(GP, A_CONV), n, a, split_lo, reduce_ada)
                    keep_mod(a, A_CONV)
                    add_halves(g, 4 * j)
                    at = Pos(j, 2, i)
                    bias = cols[:, bass.ds(value(at, 0, 4) + C_BOUT, 4)].rearrange("p (t o) -> p t o", o=1).broadcast_to([P, 4, T])
                    ve.tensor_tensor(y[:, bass.ds(value(at, 0, 4), 4), :], s0[:, :, :], bias, ALU.add).then_inc(evac_done, 1)
            looped(ve, 2, conv_out)

            def clear_y():
                step(ve.memset(y[:, :, :], 0.0))
                settled()

            ve.wait_ge(evac_done, G_MLP0)
            ve.wait_ge(ada_used, A_M0)
            residual(S_Y0, M_MIX0 + 32, C_POSTMIX)
            sum_squares(S_H1)
            scale_shift(co_a, co_b, M_MLP0, C_PREMLP)
            deviation(S_H1)
            modulated(xn, co_a, co_b, 8)
            ve.wait_ge(x_ready, 12)
            clear_y()
            mlp(ve, group, G_MLP0, N_MLP0, A_M0, A_MLP0, 0, 0)

            ve.wait_ge(evac_done, G_KR)
            ve.wait_ge(ada_used, A_ATT)
            residual(S_Y1, M_MLP0 + 32, C_POSTMLP)
            sum_squares(S_H2)
            scale_shift(co_a, co_b, M_KV, C_GKV)
            scale_shift(co_a2, co_b2, M_MIX1, C_PREMIX + NT)
            deviation(S_H2)
            modulated(xn, co_a, co_b, 12)
            ve.wait_ge(x_ready, 16)
            modulated(hid, co_a2, co_b2, 16)

            split_lo(fixed(N_KR + 2))
            b = 4 * (G_KR % 2)
            ve.wait_ge(low_copied, G_KR + 1)
            ve.tensor_tensor(s0[:, 0, :], ps[:, b, 0:T], s1[:, 0, :], ALU.add).then_inc(summed, 1)
            ve.wait_ge(summed, G_KR + 1)
            step(ve.tensor_tensor(s2[0:ROPE, 0, :], s0[0:ROPE, 0, :], table[0:ROPE, :], ALU.mult))
            step(ve.tensor_tensor(s2[0:ROPE, 1, :], s0[ROPE:P, 0, :], table[ROPE:P, :], ALU.mult))
            settled()
            ve.tensor_tensor(krope[:, :], s2[0:ROPE, 0, :], s2[0:ROPE, 1, :], ALU.add).then_inc(evac_done, 1)

            def rank_norm(k, i, gain):
                sum_squares(k)
                deviation(k)
                step(ve.tensor_tensor(quarter(y, i), quarter(y, i), wide(rstd[:, :]), ALU.mult))
                settled()
                for t in range(RT):
                    last = ve.tensor_scalar(y[:, 4 * i + t, :], y[:, 4 * i + t, :], cols[:, gain + t:gain + t + 1], None, ALU.mult)
                last.then_inc(xf_ready, 1)
                ve.wait_ge(xhi, 20 + i + 1)
                ve.tensor_tensor(xn[:, 4 * i:4 * i + 4, 1, :], quarter(y, i), xn[:, 4 * i:4 * i + 4, 0, :].bitcast(f32),
                                 ALU.subtract).then_inc(x_ready, 1)

            for i, (g, n, gain) in enumerate(((G_DKV, N_DKV, C_GCKV), (G_DQ, N_DQ, C_GCQ))):
                run_order(group_order(GP, 4), fixed(n), fixed(A_ATT + 4 * i), split_lo, reduce_ada)
                add_halves(fixed(g), 4 * (g % 2))
                ve.wait_ge(x_ready, 20)
                ve.tensor_copy(quarter(y, i), s0[:, :, :]).then_inc(evac_done, 1)
                rank_norm((S_CKV, S_CQ)[i], i, gain)

            def evac_proj(p):
                ve.wait_ge(split_used, value(p, 1, 2) + N_PAIR)
                wait(ve, scores, value(p))
                ve.tensor_copy(qn, ps[:, 2, :].rearrange("p (j n) -> p j n", j=2))
                tab = table[:, :].rearrange("p (o n) -> p o n", o=1).broadcast_to([P, 2, T])
                both = ps[:, 3, :].rearrange("p (j n) -> p j n", j=2)
                wait(ve, q_ready, value(p))
                ve.tensor_tensor(s2[0:ROPE, 0:2, :], both[0:ROPE], tab[0:ROPE], ALU.mult).then_inc(q_step, 1)
                ve.tensor_tensor(s2[0:ROPE, 2:4, :], both[ROPE:P], tab[ROPE:P], ALU.mult).then_inc(q_step, 1)
                ve.wait_ge(q_step, value(p, 1, 2))
                ve.tensor_tensor(qr, s2[0:ROPE, 0:2, :], s2[0:ROPE, 2:4, :], ALU.add).then_inc(q_ready, 1)

            def pair(p, n, a, more):
                run_order(group_order(2, 2), n, a, split_lo, reduce_ada)
                keep_mod(a, 2)
                ve.wait_ge(scores, value(p, 1))
                wait(ve, turned, value(p))
                ve.tensor_tensor(pr, ps[:, 4:6, 0:3 * P], mask.broadcast_to([P, 2, 3 * P]), ALU.add).then_inc(masked, 1)
                ve.wait_ge(masked, value(p, 1))
                ve.tensor_reduce(stat[:, 0, :, 0], pr[:, :, 0:P], AX.X, ALU.max)
                ve.tensor_reduce(stat[:, 0, :, 1], pr[:, :, P:3 * P], AX.X, ALU.max).then_inc(maxed, 1)
                ve.wait_ge(maxed, value(p, 0, 2) + 1)
                ve.tensor_scalar(stat[:, 0, :, :], stat[:, 0, :, :], -SCALE, None, ALU.mult).then_inc(maxed, 1)
                ve.wait_ge(exps, value(p, 1))
                ve.reciprocal(stat[:, 2, :, :], stat[:, 1, :, :]).then_inc(prob_step, 1)
                ve.wait_ge(prob_step, value(p, 0, 2) + 1)
                for j in range(2):
                    for t in range(2):
                        lo, hi = (0, P) if t == 0 else (P, 3 * P)
                        last = ve.tensor_scalar(pr[:, j, lo:hi], pr[:, j, lo:hi], stat[:, 2, j, t:t + 1], None, ALU.mult)
                last.then_inc(prob_step, 1)
                if more:
                    evac_proj(ahead(p, 1))
                ve.wait_ge(o_hi, value(p, 1))
                at = bass.ds(value(p, 0, 2), 2)
                ve.tensor_tensor(hid[:, at, 1, :], ps[:, 4, :].rearrange("p (j n) -> p j n", j=2), hid[:, at, 0, :].bitcast(f32),
                                 ALU.subtract).then_inc(o_ready, 1)

            evac_proj(fixed(0))
            looped(ve, 3, lambda i: [pair(Pos(k, 2, i), Pos(N_PAIR + 2 * k, 4, i), Pos(A_PAIR + 2 * k, 4, i), True)
                                     for k in range(2)])
            pair(fixed(6), fixed(N_PAIR + 12), fixed(A_PAIR + 12), True)
            pair(fixed(7), fixed(N_PAIR + 14), fixed(A_PAIR + 14), False)

            def wo(i):
                for j in range(2):
                    g, n = Pos(G_WO + j, 2, i), Pos(N_WO + GP * j, 2 * GP, i)
                    a = Pos(A_WO + 6 * j, 12, i)
                    run_order(group_order(GP, 6), n, a, split_lo, reduce_ada)
                    keep_mod(a, 6)
                    add_halves(g, 4 * ((G_WO + j) % 2))
                    ve.tensor_copy(y[:, bass.ds(value(Pos(j, 2, i), 0, 4), 4), :], s0[:, :, :]).then_inc(evac_done, 1)
            looped(ve, 2, wo)

            ve.wait_ge(evac_done, G_MLP1)
            ve.wait_ge(ada_used, M_ALL)
            residual(S_Y2, M_MIX1 + 32, C_POSTMIX + NT)
            sum_squares(S_H3)
            scale_shift(co_a, co_b, M_MLP1, C_PREMLP + NT)
            deviation(S_H3)
            modulated(xn, co_a, co_b, 22)
            ve.wait_ge(x_ready, 26)
            clear_y()
            mlp(ve, group, G_MLP1, N_MLP1, 0, 0, 16, 1)
            ve.wait_ge(evac_done, G_MLP1 + 8 * CHUNKS)
            residual(S_Y3, M_MLP1 + 32, C_POSTMLP + NT)

        @block.tensor
        def _(pe):
            def product(g, n, src, ready, at):
                b = 4 * (g.static % 2)
                wait(pe, summed, value(g, -1))
                for j in range(GP):
                    if ready is not None:
                        pe.wait_ge(ready, at + j + 1)
                    pe.wait_ge(lo_ready, value(n, j + 1))
                    d = (n.static + j) % 2
                    for k in range(4):
                        for o in range(GT):
                            at_w = slice((k * GT + o) * P, (k * GT + o + 1) * P)
                            kt = 4 * j + k
                            first, end = kt == 0, kt == NT - 1

                            def high():
                                return pe.matmul(ps[:, b + o, :], wsp[:, d, 0, at_w], src[:, kt, :, :].rearrange("p a n -> p (a n)"), start=first, stop=end)

                            def low():
                                return pe.matmul(ps[:, b + o, 0:T], wsp[:, d, 1, at_w], src[:, kt, 0, :], start=False, stop=False)
                            if first:
                                high()
                                last = low()
                            else:
                                low()
                                last = high()
                    last.then_inc(split_used, 1)

            def reduce_over_features(k, seen=0):
                for q in range(QUARTERS[k]):
                    pe.wait_ge(partial, sbase[k] + q + 1)
                    last = pe.matmul(ps[:, stat_bank(k), 0:T], ones[:, :], s2[:, q, :], start=q == 0, stop=q == QUARTERS[k] - 1)
                last.then_inc(total, 1)

            def group(kind, g, n, a, per, t, u, j):
                if kind == "up":
                    product(g, n, xn, None, 0)
                else:
                    product(g, n, hid, hid_ready, value(u))

            reduce_over_features(S_H0)

            def conv_in(i):
                for j in range(2):
                    product(Pos(G_IN + j, 2, i), Pos(N_IN + GP * j, 2 * GP, i), xn, x_ready, 0)
            looped(pe, 4, conv_in)
            reduce_over_features(S_MU)
            reduce_over_features(S_VAR)

            def conv_out(i):
                for j in range(2):
                    product(Pos(G_OUT + j, 2, i), Pos(N_OUT + GP * j, 2 * GP, i), hid, x_ready, 4)
            looped(pe, 2, conv_out)
            reduce_over_features(S_Y0)
            reduce_over_features(S_H1)
            pe.wait_ge(x_ready, 12)
            mlp(pe, group, G_MLP0, N_MLP0, 0, 0, 0, 0)
            reduce_over_features(S_Y1)
            reduce_over_features(S_H2)

            pe.wait_ge(x_ready, 16)
            pe.wait_ge(lo_ready, N_KR + 1)
            b, d = 4 * (G_KR % 2), N_KR % 2
            for kt in range(NT):
                at_w = slice(kt * P, (kt + 1) * P)
                if kt:
                    pe.matmul(ps[:, b, 0:T], wsp[:, d, 1, at_w], xn[:, kt, 0, :], start=False, stop=False)
                last = pe.matmul(ps[:, b, :], wsp[:, d, 0, at_w], xn[:, kt, :, :].rearrange("p a n -> p (a n)"), start=kt == 0, stop=kt == NT - 1)
                if not kt:
                    last = pe.matmul(ps[:, b, 0:T], wsp[:, d, 1, at_w], xn[:, kt, 0, :], start=False, stop=False)
            last.then_inc(split_used, 1)
            product(fixed(G_DKV), fixed(N_DKV), xn, None, 0)
            reduce_over_features(S_CKV)
            product(fixed(G_DQ), fixed(N_DQ), hid, x_ready, 16)
            reduce_over_features(S_CQ)

            def project(p, n):
                wait(pe, kv_copied, value(p))
                wait(pe, q_ready, value(p))
                pe.wait_ge(x_ready, 22)
                d = n.static % 2
                pe.wait_ge(lo_ready, value(n, 1))

                def three(bank, at, w_at, src, width=T):
                    for kt in range(RT):
                        wa = slice(kt * 512 + w_at, kt * 512 + w_at + P)
                        pairs3 = ((0, 0), (0, 1), (1, 0))
                        for m, (wi, xi) in enumerate(pairs3):
                            last = pe.matmul(ps[:, bank, at:at + T], wsp[:, dd, wi, wa], src[:, kt, xi, :],
                                             start=kt == 0 and m == 0, stop=kt == RT - 1 and m == 2)
                    return last
                dd = d
                ckv, cq = xn[:, 0:RT], xn[:, RT:2 * RT]
                for j in range(2):
                    three(0, T * j, P * j, ckv)
                for tt in range(2):
                    for kt in range(RT):
                        wa = slice(kt * 512 + 2 * P, kt * 512 + 4 * P)
                        for m, (wi, xi) in enumerate(((0, 0), (0, 1), (1, 0))):
                            last = pe.matmul(ps[:, 1, T * tt:T * tt + T], ckv[:, kt, xi, P * tt:P * tt + P], wsp[:, d, wi, wa],
                                             start=kt == 0 and m == 0, stop=kt == RT - 1 and m == 2)
                last.then_inc(split_used, 1)
                pe.wait_ge(lo_ready, value(n, 2))
                dd = (n.static + 1) % 2
                for j in range(2):
                    three(2, T * j, 2 * P * j, cq)
                for j in range(2):
                    last = three(3, T * j, 2 * P * j + P, cq)
                last.then_inc(split_used, 1)

            def score(p):
                pe.wait_ge(kv_copied, value(p, 1))
                pe.wait_ge(q_ready, value(p, 1))
                wait(pe, o_ready, value(p))
                for j in range(2):
                    for t in range(2):
                        at, keys = (0, P) if t == 0 else (P, T)
                        pe.matmul(ps[:, 4 + j, at:at + keys], qn[:, j, P * t:P * t + P], kn[:, j, 0:keys], start=True, stop=False)
                        last = pe.matmul(ps[:, 4 + j, at:at + keys], qr[:, j, P * t:P * t + P], krope[:, 0:keys], start=False, stop=True)
                last.then_inc(scores, 1)

            def attend(p):
                b = p.static % 2
                pe.wait_ge(prob_step, value(p, 1, 2))
                wait(pe, prt_ready, value(p))
                for j in range(2):
                    for k in range(3):
                        last = pe.transpose(ps[:, 6 + j, P * k:P * k + P], pr[:, j, P * k:P * k + P], ident)
                last.then_inc(turned, 1)
                pe.wait_ge(prt_ready, value(p, 1))
                for j in range(2):
                    pe.matmul(ps[:, 4, T * j:T * j + T], vv[:, b, 0, P * j:P * j + P], prt[:, j, 0:T], start=True, stop=False)
                    last = pe.matmul(ps[:, 4, T * j + P:T * j + T], vv[:, b, 1, P * j:P * j + P], prt[:, j, T:T + P], start=False, stop=True)
                last.then_inc(o_done, 1)

            project(fixed(0), fixed(N_PAIR))

            def pair(p, n, more):
                score(p)
                if more:
                    project(ahead(p, 1), ahead(n, 2))
                attend(p)
            looped(pe, 3, lambda i: [pair(Pos(k, 2, i), Pos(N_PAIR + 2 * k, 4, i), True) for k in range(2)])
            pair(fixed(6), fixed(N_PAIR + 12), True)
            pair(fixed(7), None, False)

            pe.wait_ge(o_ready, HEADS // 2)

            def wo(i):
                for j in range(2):
                    product(Pos(G_WO + j, 2, i), Pos(N_WO + GP * j, 2 * GP, i), hid, None, 0)
            looped(pe, 2, wo)
            reduce_over_features(S_Y2)
            reduce_over_features(S_H3)
            pe.wait_ge(x_ready, 26)
            mlp(pe, group, G_MLP1, N_MLP1, 0, 0, 16, 1)
            reduce_over_features(S_Y3)


def _tiles(w):
    k, n = w.shape
    return w.reshape(k // P, P, n // P, P).transpose(0, 2, 1, 3)


def _group(w, tiles):
    t = _tiles(w)[:, tiles]
    kt = t.shape[0]
    return t.reshape(kt // 4, 4, 4, P, P).transpose(0, 3, 1, 2, 4).reshape(kt // 4, P, PIECE)


def _streams(a):
    w = []

    def groups(m):
        for n in range(m.shape[1] // (GT * P)):
            w.append(_group(m, list(range(GT * n, GT * n + GT))))

    def mlp(l):
        for ch in range(CHUNKS):
            groups(a["mlp_w_up"][l][:, ch * D:(ch + 1) * D])
            groups(a["mlp_w_down"][l][ch * D:(ch + 1) * D])
    for g in range(8):
        w.append(_group(a["conv_w_in"][0], [2 * g, 2 * g + 1, NT + 2 * g, NT + 2 * g + 1]))
    groups(a["conv_w_out"][0])
    mlp(0)
    kr = a["w_kr"]
    kr = np.concatenate([kr, kr[:, ROPE // 2:], kr[:, :ROPE // 2]], axis=1)
    w.append(kr.reshape(NT, P, P).transpose(1, 0, 2).reshape(1, P, PIECE))
    groups(a["w_dkv"])
    groups(a["w_dq"][0])
    uk = a["w_uk"].reshape(RT, P, HEADS // 2, 2 * NOPE)
    uv = a["w_uv"].reshape(RT, P, HEADS // 2, 2 * VDIM)
    kv = np.concatenate([uk, uv], axis=3).transpose(2, 1, 0, 3).reshape(HEADS // 2, 1, P, PIECE)
    uq = a["w_uq"][0].reshape(RT, P, HEADS // 2, 2, NOPE + ROPE)
    half = NOPE + ROPE // 2
    uq = np.concatenate([uq, uq[..., half:], uq[..., NOPE:half]], axis=4)
    uq = uq.transpose(2, 1, 0, 3, 4).reshape(HEADS // 2, 1, P, PIECE)
    w.append(np.concatenate([kv, uq], axis=1).reshape(HEADS, P, PIECE))
    groups(a["w_o"][0])
    mlp(1)
    ada = [a["w_ada_mix"][0], a["w_ada_mlp"][0], a["w_ada_kv"], a["w_ada_mix"][1], a["w_ada_mlp"][1]]
    ada = np.concatenate([m.T.reshape(-1, P, D) for m in ada])
    return np.concatenate(w), ada


def _columns(a):
    def col(v):
        return np.asarray(v).reshape(-1, P).T
    bada = [a["b_ada_mix"][0], a["b_ada_mlp"][0], a["b_ada_kv"], a["b_ada_mix"][1], a["b_ada_mlp"][1]]
    b_in = a["conv_b_in"][0].reshape(2, 8, 2, P).transpose(1, 0, 2, 3)
    dw = np.concatenate([a["conv_dw"][0], a["conv_dw_b"][0][None]]).reshape(WIDTH + 1, NT, P).transpose(1, 0, 2)
    parts = [*bada, a["g_pre_mix"], a["g_post_mix"], a["g_pre_mlp"], a["g_post_mlp"], b_in, dw,
             a["conv_ln_g"], a["conv_ln_b"], a["conv_b_out"], a["g_kv"], a["g_ckv"], a["g_cq"]]
    return np.ascontiguousarray(np.concatenate([col(v) for v in parts], axis=1))


def _constants():
    k = np.zeros((P, K_ALL), np.float32)
    inv = 1.0 / (np.float32(THETA) ** (np.arange(0, ROPE, 2, dtype=np.float32) / np.float32(ROPE)))
    k[:, K_INV] = np.tile(inv.astype(np.float32), 4)
    k[:, K_SIGN] = np.where(np.arange(P) % ROPE < ROPE // 2, -1.0, 1.0)
    k[:, K_IDENT:K_IDENT + P] = np.eye(P)
    tri = np.where(np.arange(P)[None, :] <= np.arange(P)[:, None], 0.0, NEG)
    k[:, K_MASK:K_MASK + P] = tri
    k[:, K_MASK + 2 * P:] = tri
    return k


def kernel(**inputs):
    import concourse.bacc as _bacc
    from concourse.bass_utils import run_bass_kernel_spmd as _run

    a = {k: np.asarray(v) for k, v in inputs.items()}
    w, ada = _streams(a)
    arrays = {
        "x_t": np.ascontiguousarray(a["x"][0].T.reshape(NT, P, T).transpose(1, 0, 2)),
        "c": a["c"][0],
        "positions": a["positions"][0],
        "columns": _columns(a),
        "constants": _constants(),
        "w_stream": w,
        "ada_stream": ada,
    }
    nc = _bacc.Bacc("TRN2", target_bir_lowering=False, num_devices=1, dynamic_dma_scratch_size=1024)
    args = [nc.dram_tensor(n, v.shape, mybir.dt.from_np(v.dtype), kind="ExternalInput").ap() for n, v in arrays.items()]
    out = nc.dram_tensor("out_t", (P, NT, T), mybir.dt.float32, kind="ExternalOutput").ap()
    trunk(nc, *args, out)
    r = _run(nc, [arrays], core_ids=[0])
    got = r.results[0]["out_t"]
    return np.ascontiguousarray(np.asarray(got).transpose(1, 0, 2).reshape(D, T).T)[None]
```

```python
from collections import namedtuple
from contextlib import ExitStack

import concourse.bass as bass
import numpy as np
from concourse import mybir

P = 128
D = 2048
T = 256
NT = D // P
WIDTH = 31
HEADS, NOPE, ROPE, VDIM, RANK = 16, 128, 64, 128, 512
RT = RANK // P
FF = 4 * D
CHUNKS = FF // D
THETA = 10000.0
EPS = 1e-6
SCALE = float(NOPE + ROPE) ** -0.5
NEG = -1e30
PIECE = 2048
GT = 4
GP = NT // 4

G_OUT, G_MLP0 = 0, 4
G_DQ = G_MLP0 + 2 * GT * CHUNKS
G_KR, G_DKV, G_WO = G_DQ + 1, G_DQ + 2, G_DQ + 3
G_MLP1 = G_WO + 4
N_IN, N_OUT, N_MLP0 = 0, 32, 48
N_DQ = N_MLP0 + 8 * GP * CHUNKS
N_KR = N_DQ + GP
N_DKV = N_KR + 1
N_PAIR = N_DKV + GP
N_WO = N_PAIR + HEADS
N_MLP1 = N_WO + 4 * GP
N_ALL = N_MLP1 + 8 * GP * CHUNKS

M_MIX0, M_MLP0, M_KV, M_MIX1, M_MLP1 = 0, 48, 96, 128, 176
M_ALL = 224
IN_GROUPS = 2 * NT // GT
START_GROUPS = 4
PE_TAPS = 14
A_START, A_CONV, A_UP, A_DOWN = 32, 4, 2, 3
A_IN, A_LN, A_OUT, A_M0 = 32, 64, 68, 80
A_OUT_GROUP = 3
A_DKV = A_M0 + GT * (CHUNKS * (A_UP + A_DOWN) + 1)
A_PAIR = A_DKV + 4
A_PER_PAIR, A_WO_GROUP = 3, 4
A_WO = A_PAIR + A_PER_PAIR * HEADS // 2
A_M1 = A_WO + 4 * A_WO_GROUP

C_BADA = 0
C_PREMIX, C_POSTMIX, C_PREMLP, C_POSTMLP = 224, 256, 288, 320
C_CONV = 352
CONV = GT + 2 * (WIDTH + 1)
C_LNG = C_CONV + IN_GROUPS * CONV
C_LNB, C_BOUT, C_GKV = C_LNG + 16, C_LNG + 32, C_LNG + 48
C_GCKV, C_GCQ = C_LNG + 64, C_LNG + 68
C_ALL = C_LNG + 72
K_INV, K_SIGN, K_IDENT, K_MASK = 0, 1, 2, 130
K_ALL = K_MASK + 3 * P

S_H0, S_MU, S_VAR, S_Y0, S_H1, S_Y1, S_H2, S_CQ, S_CKV, S_Y2, S_H3, S_Y3 = range(12)
SQUARES = [4, 0, 4, 4, 4, 4, 4, 1, 1, 4, 4, 4]
BATCHES = [4, 1, 4, 1, 4, 1, 4, 1, 1, 1, 4, 1]
PARTIALS = [0, 0, 0, 3, 0, 3, 0, 0, 0, 3, 0, 3]

Pos = namedtuple("Pos", "static loops")


def at_loop(n, *loops):
    return Pos(n, tuple(x for x in loops if x[1] is not None))


def fixed(n):
    return Pos(n, ())


def ahead(p, k):
    return Pos(p.static + k, p.loops)


def value(p, plus=0, times=1):
    n = times * (p.static + plus)
    for step, reg in p.loops:
        n = n + times * step * reg
    return n


def turn(p, ring):
    return Pos(p.static // ring, tuple((step // ring, reg) for step, reg in p.loops))


def wait(eng, sem, v):
    if not (isinstance(v, int) and v <= 0):
        eng.wait_ge(sem, v)


def trunk(nc, x_t, c, pos, cols_d, consts_d, w_stream, ada_stream, out_t):
    f32, f32r, i32 = mybir.dt.float32, mybir.dt.float32r, mybir.dt.int32
    ALU, ACT, AX = mybir.AluOpType, mybir.ActivationFunctionType, mybir.AxisListType
    ctx = ExitStack()
    with ctx:
        def sb(name, shape, dt=f32):
            return ctx.enter_context(nc.sbuf_tensor(name, shape, dt))

        def sem(name):
            return ctx.enter_context(nc.semaphore(name))

        h = sb("h", [P, NT, T])
        with (nc.sbuf_tensor("diag0", [P, 2, PE_TAPS, P], f32) as diag0, nc.sbuf_tensor("xn_end", [P, NT * T * 2 - 2 * PE_TAPS * P], f32),
              nc.sbuf_tensor("xf", [P, NT, T], f32) as xf, nc.sbuf_tensor("diag1", [P, 2, PE_TAPS, P], f32) as diag1):
            diag = (diag0, diag1)
        xn = sb("xn", [P, NT, 2, T], f32r)
        hid = sb("hid", [P, NT, 2, T], f32r)
        y = sb("y", [P, NT, T])
        raw = sb("raw", [P, 4, PIECE])
        wsp = sb("wsp", [P, 2, 2, PIECE], f32r)
        ada = sb("ada", [P, 2, PIECE])
        cb = sb("cb", [P, D])
        s0 = sb("s0", [P, 4, T])
        s1 = sb("s1", [P, 4, T])
        s2 = sb("s2", [P, 4, T])
        s3 = sb("s3", [P, 4, T])
        root = sb("root", [P, T])
        rstd = sb("rstd", [P, T])
        mod = sb("mod", [P, M_ALL])
        mod_step = sb("mod_step", [P, 8])
        cols = sb("cols", [P, C_ALL])
        consts = sb("consts", [P, K_ALL])
        co_a = sb("co_a", [P, NT])
        co_b = sb("co_b", [P, NT])
        co_a2 = sb("co_a2", [P, NT])
        co_b2 = sb("co_b2", [P, NT])
        co_g = sb("co_g", [P, NT])
        epsc = sb("epsc", [P, 2])
        scratch = sb("scratch", [P, 1])
        ones = sb("ones", [P, P])
        posi = sb("posi", [P, T], i32)
        table = sb("table", [P, T])
        krope = sb("krope", [ROPE, T])
        ubuf = sb("ubuf", [P, 4, 2, WIDTH - 1 + T])
        stat = sb("stat", [P, 3, 2, 2])
        ps = ctx.enter_context(nc.psum_tensor("ps", [P, 8, 512], f32))

        yw = y[:, :, :].rearrange("p t n -> p (t n)")
        qn = yw[:, 0:512].rearrange("p (j n) -> p j n", j=2)
        qr = yw[0:ROPE, 512:1024].rearrange("p (j n) -> p j n", j=2)
        kn = yw[:, 1024:1536].rearrange("p (j n) -> p j n", j=2)
        vv = yw[:, 1536:2560].rearrange("p (b k n) -> p b k n", b=2, k=2)
        pr = yw[:, 2560:3328].rearrange("p (j n) -> p j n", j=2)
        prt = yw[:, 3328:4096].rearrange("p (j n) -> p j n", j=2)
        cq, ckv = hid[:, NT - RT:NT], xn[:, 0:RT]
        ident = consts[:, K_IDENT:K_IDENT + P]
        mask = consts[:, K_MASK:K_MASK + 3 * P].rearrange("p (o n) -> p o n", o=1)

        small_loaded, c_loaded = sem("small_loaded"), sem("c_loaded")
        h_loaded = [sem(f"h_loaded{q}") for q in range(4)]
        w_loaded = [sem(f"w_loaded{s}") for s in range(4)]
        ada_loaded = [sem(f"ada_loaded{s}") for s in range(2)]
        ada_used = sem("ada_used")
        mod_kept = sem("mod_kept")
        c_ready = sem("c_ready")
        hi_ready = sem("hi_ready")
        lo_ready = sem("lo_ready")
        split_used = sem("split_used")
        low_copied = sem("low_copied")
        summed = sem("summed")
        evac_done = sem("evac_done")
        hid_hi = sem("hid_hi")
        hid_ready = sem("hid_ready")
        native_used = sem("native_used")
        diag_ready = sem("diag_ready")
        pe_taps = sem("pe_taps")
        conv_done = sem("conv_done")
        xin_ready = sem("xin_ready")
        sig_ready = sem("sig_ready")
        u_ready = sem("u_ready")
        taps = sem("taps")
        squares = sem("squares")
        partial = sem("partial")
        total = sem("total")
        root_ready = sem("root_ready")
        rstd_ready = sem("rstd_ready")
        y_scaled = sem("y_scaled")
        gates_ready = sem("gates_ready")
        start_normed = sem("start_normed")
        coef_ready = sem("coef_ready")
        centred = sem("centred")
        scaled = sem("scaled")
        silu_done = sem("silu_done")
        h_ready = sem("h_ready")
        xf_ready = sem("xf_ready")
        xhi = sem("xhi")
        x_ready = sem("x_ready")
        step_done = sem("step_done")
        trig = sem("trig")
        ang = sem("ang")
        kv_copied = sem("kv_copied")
        q_copied = sem("q_copied")
        q_ready = sem("q_ready")
        q_step = sem("q_step")
        scores = sem("scores")
        masked = sem("masked")
        maxed = sem("maxed")
        exps = sem("exps")
        sums_inverted = sem("sums_inverted")
        probs_ready = sem("probs_ready")
        turned = sem("turned")
        prt_ready = sem("prt_ready")
        o_done = sem("o_done")
        o_hi = sem("o_hi")
        o_ready = sem("o_ready")
        y_cleared = sem("y_cleared")
        stored = sem("stored")

        def banks_of(g):
            return 4 * (g % 2)
        sum_bank = {S_H0: 6, S_MU: 6, S_VAR: 6, S_CQ: 5, S_CKV: 5}
        for y_sum, h_sum, g_next in ((S_Y0, S_H1, G_MLP0), (S_Y1, S_H2, G_DQ), (S_Y2, S_H3, G_MLP1), (S_Y3, None, G_MLP1 + 8 * CHUNKS)):
            sum_bank[y_sum], sum_bank[h_sum] = banks_of(g_next), banks_of(g_next - 1)
        LAST_OF = {G_MLP0: S_Y0, G_DQ: S_Y1, G_MLP1: S_Y2, G_MLP1 + 8 * CHUNKS: S_Y3}

        def before(counts, k):
            return sum(counts[:k])

        def inverses(k):
            return k + 1 if k < S_MU else k

        def in_bank(g):
            return 2 * g if g < START_GROUPS else 2 * (g % 2)

        def product_end(g):
            return GP * (START_GROUPS - 1) + g + 1 if g < START_GROUPS else GP * (g + 1)

        TAP_BANKS = (4, 5, 7, 4, 5, 7, 0, 2)

        LOAD_LEAD = 4

        def group_order(pieces, adas, lead=2):
            out = []
            for k in range(pieces):
                out.append(("w", k + lead))
                if k < 2:
                    out += [("a", a) for a in (range(adas // 2) if k == 0 else range(adas // 2, adas))]
            return out

        def run_order(order, p, a, do_w, do_a):
            for kind, k in order:
                if kind == "w":
                    if p.loops or p.static + k < N_ALL:
                        do_w(ahead(p, k))
                else:
                    do_a(ahead(a, k))

        def looped(eng, count, body):
            body(None)
            with eng.Fori(1, count) as i:
                body(i)

        def mlp(eng, group, g0, n0, a0, ups, downs, last_ups, u0):
            per = 4 * (ups + downs)

            def two(kind, c, i, u):
                off, a_off, adas = (0, 0, ups) if kind == "up" else (4, 4 * ups, downs)
                for j in range(2):
                    k = off + j
                    group(kind, at_loop(g0 + k, (8, c), (2, i)), at_loop(n0 + GP * k, (8 * GP, c), (2 * GP, i)),
                          at_loop(a0 + a_off + adas * j, (per, c), (2 * adas, i)), adas, at_loop(j, (2, i)), u, None)

            with eng.Fori(0, CHUNKS - 1) as c:
                with eng.Fori(0, 2) as i:
                    two("up", c, i, at_loop(u0, (4, c)))
                with eng.Fori(0, 2) as i:
                    two("down", c, i, at_loop(u0, (4, c)))
            k, ups = CHUNKS - 1, last_ups
            g0, n0, a0, u = g0 + 8 * k, n0 + 8 * GP * k, a0 + per * k, fixed(u0 + 4 * k)
            with eng.Fori(0, 2) as i:
                two("up", None, i, u)
            for k in range(4):
                group("down", fixed(g0 + 4 + k), fixed(n0 + GP * (4 + k)), fixed(a0 + 4 * ups + downs * k), downs, fixed(k), u, k)

        block = ctx.enter_context(nc.Block())

        @block.sync
        def _(sp):
            def load_w(p):
                s, n = p.static % 4, p.static
                if not p.loops and n < 4:
                    sp.wait_ge(ada_used, n + 3)
                elif n - 4 < N_OUT:
                    sp.wait_ge(native_used, value(p, -3))
                else:
                    sp.wait_ge(lo_ready, value(p, -3 - N_OUT, 2))
                sp.dma_start(raw[:, s, :], w_stream[value(p)]).then_inc(w_loaded[s], 16)

            def load_a(a):
                s = a.static % 2
                sp.wait_ge(ada_used, value(a, -1))
                sp.dma_start(ada[:, s, :], ada_stream[value(a)]).then_inc(ada_loaded[s], 16)

            def load_start(a):
                if 2 <= a < 6:
                    sp.dma_start(raw[:, a - 2, :], ada_stream[a]).then_inc(w_loaded[a - 2], 16)
                else:
                    if a >= 6:
                        sp.wait_ge(ada_used, a - 5 if a < 8 else a - 1)
                    sp.dma_start(ada[:, a % 2, :], ada_stream[a]).then_inc(ada_loaded[a % 2], 16)

            sp.dma_start(cb[:, :], c.rearrange("(o n) -> o n", o=1).broadcast_to([P, D])).then_inc(c_loaded, 16)
            sp.dma_start(cols[:, :], cols_d).then_inc(small_loaded, 16)
            sp.dma_start(consts[:, :], consts_d).then_inc(small_loaded, 16)
            sp.dma_start(posi[:, :], pos.rearrange("(o n) -> o n", o=1).broadcast_to([P, T])).then_inc(small_loaded, 16)
            for q in range(5):
                for k in range(8):
                    if q < 4:
                        load_start(8 * q + k)
                        if q == 0 and k % 2:
                            sp.dma_start(h[:, 2 * k - 2:2 * k + 2, :], x_t[:, 2 * k - 2:2 * k + 2, :]).then_inc(h_loaded[k // 2], 16)
                    if q and k % 2:
                        load_w(fixed(4 * (q - 1) + k // 2))

            def group(kind, g, n, a, per, t, u, q):
                run_order(group_order(GP, per, LOAD_LEAD), n, a, load_w, load_a)

            for k in range(IN_GROUPS):
                order = [x for x in group_order(GP, A_CONV, 0) if x[0] == "a" or k < IN_GROUPS - START_GROUPS]
                run_order(order, fixed(N_IN + GP * (START_GROUPS + k)), fixed(A_IN + A_CONV * k), load_w, load_a)
            for k in range(LOAD_LEAD):
                load_w(fixed(N_OUT + k))
            for k in range(A_OUT - A_LN):
                load_a(fixed(A_LN + k))
            for k in range(4):
                group("out", None, fixed(N_OUT + GP * k), fixed(A_OUT + A_OUT_GROUP * k), A_OUT_GROUP, fixed(k), None, k)
            mlp(sp, group, G_MLP0, N_MLP0, A_M0, A_UP, A_DOWN, A_UP + 1, 0)
            run_order(group_order(GP, 0, LOAD_LEAD), fixed(N_DQ), None, load_w, load_a)
            run_order(group_order(1, 0, LOAD_LEAD), fixed(N_KR), None, load_w, load_a)
            run_order(group_order(GP, 4, LOAD_LEAD), fixed(N_DKV), fixed(A_DKV), load_w, load_a)

            def pairs(i, off):
                for k in range(2):
                    run_order(group_order(2, A_PER_PAIR, LOAD_LEAD), at_loop(N_PAIR + 4 * off + 2 * k, (4, i)),
                              at_loop(A_PAIR + A_PER_PAIR * (2 * off + k), (2 * A_PER_PAIR, i)), load_w, load_a)
            looped(sp, 3, lambda i: pairs(i, 0))
            pairs(None, 3)

            for k in range(4):
                group("wo", None, fixed(N_WO + GP * k), fixed(A_WO + A_WO_GROUP * k), A_WO_GROUP, fixed(k), None, k)
            mlp(sp, group, G_MLP1, N_MLP1, A_M1, 1, 0, 1, 16)
            for q in range(4):
                sp.wait_ge(h_ready, 12 + q + 1)
                sp.dma_start(out_t[:, 4 * q:4 * q + 4, :], h[:, 4 * q:4 * q + 4, :]).then_inc(stored, 16)
            sp.wait_ge(stored, 64)

        @block.scalar
        def _(act):
            def split_hi(p):
                s, d = p.static % 4, p.static % 2
                act.wait_ge(w_loaded[s], value(turn(p, 4), 2, 16))
                for half in range(2):
                    at = slice(half * PIECE // 2, (half + 1) * PIECE // 2)
                    wait(act, split_used, value(p, -N_OUT, 2) - 3 + half)
                    act.activation(wsp[:, d, 0, at], raw[:, s, at], ACT.Copy).then_inc(hi_ready, 1)

            def halves(g, n, b, tiles=4, pieces=GP):
                act.wait_ge(split_used, value(n, pieces - N_OUT, 2))
                wait(act, summed, value(g))
                act.activation(s1[:, 0:tiles, :], ps[:, b:b + tiles, T:2 * T], ACT.Copy).then_inc(low_copied, 1)

            def quarter(buf, q):
                return buf[:, 4 * q:4 * q + 4, :]

            def square_y(k, q, g):
                act.wait_ge(evac_done, g + 1)
                wait(act, partial, before(PARTIALS, k) + q)
                act.activation(s3[:, :, :], quarter(y, q), ACT.Square).then_inc(squares, 1)
                act.wait_ge(squares, before(SQUARES, k) + q + 1)
                act.wait_ge(gates_ready, {S_Y0: 1, S_Y1: 2, S_Y2: 3, S_Y3: 4}[k])
                for t in range(4 * q, 4 * q + 4):
                    last = act.activation(y[:, t, :], y[:, t, :], ACT.Copy, scale=co_g[:, t:t + 1])
                last.then_inc(y_scaled, 1)

            def group(kind, g, n, a, per, t, u, q):
                order = group_order(GP, 0)
                late = order[-1:] if q == 3 else []
                run_order(order[:len(order) - len(late)], n, a, split_hi, None)
                halves(g, n, 4 * (g.static % 2))
                run_order(late, n, a, split_hi, None)
                if kind == "up":
                    act.wait_ge(evac_done, value(g, 1))
                    act.activation(hid[:, bass.ds(value(t, 0, 4), 4), 0, :], s2[:, :, :], ACT.Copy).then_inc(hid_hi, 1)
                elif q is not None:
                    square_y(LAST_OF[g.static - q + 4], q, g.static)

            def square(k, q, src, ready, at):
                act.wait_ge(ready, at)
                wait(act, total, before(BATCHES, k) + q - 1)
                act.activation((s3, s0)[q % 2][:, :, :], src, ACT.Square).then_inc(squares, 1)

            def load_root_table():
                act.activation(scratch[:, :], epsc[:, 0:1], ACT.Sqrt)

            def take_root(k, n):
                act.wait_ge(total, before(BATCHES, k + 1))
                wait(act, rstd_ready, inverses(k - 1) if k else 0)
                act.activation(root[:, :], ps[:, sum_bank[k], 0:T], ACT.Sqrt, bias=epsc[:, 0:1], scale=1.0 / n).then_inc(root_ready, 1)

            def shifted(dst, cb_, i):
                for q in range(4):
                    act.wait_ge(xf_ready, i + q + 1)
                    for t in range(4 * q, 4 * q + 4):
                        last = act.activation(dst[:, t, 0, :], y[:, t, :], ACT.Identity, bias=cb_[:, t:t + 1])
                    last.then_inc(xhi, 1)

            act.wait_ge(c_loaded, 16)
            act.activation(cb[:, :], cb[:, :], ACT.Silu).then_inc(c_ready, 1)
            act.wait_ge(ang, 1)
            act.activation(table[64:128, :], rstd[64:128, :], ACT.Sin, scale=consts[64:128, K_SIGN:K_SIGN + 1]).then_inc(trig, 1)
            act.wait_ge(ang, 2)
            act.activation(table[0:64, :], root[0:64, :], ACT.Sin, scale=-1.0, bias=epsc[0:64, 1:2]).then_inc(trig, 1)
            for q in range(4):
                square(S_H0, q, quarter(h, q), h_loaded[q], 16)
            take_root(S_H0, D)

            def diagonals(g):
                wait(act, pe_taps, g - 1)
                for t in range(2):
                    for w in range(PE_TAPS):
                        c0 = C_CONV + CONV * g + GT + t * (WIDTH + 1) + w
                        made = act.activation(diag[g % 2][:, t, w, :], ident, ACT.Copy, scale=cols[:, c0:c0 + 1])
                made.then_inc(diag_ready, 1)

            def gate_half(g):
                wait(act, native_used, product_end(g))
                wait(act, u_ready, g - 1)
                for t in range(2):
                    c0 = C_CONV + CONV * g + 2 + t
                    last = act.activation(s1[:, 2 * (g % 2) + t, :], ps[:, in_bank(g) + 1, T * t:T * t + T], ACT.Sigmoid,
                                          bias=cols[:, c0:c0 + 1])
                last.then_inc(sig_ready, 1)

            for q in range(4):
                act.wait_ge(start_normed, q + 1)
                act.wait_ge(coef_ready, q + 1)
                for t in range(4 * q, 4 * q + 4):
                    last = act.activation(xf[:, t, :], y[:, t, :], ACT.Identity, scale=co_a[:, t:t + 1], bias=co_b[:, t:t + 1])
                last.then_inc(xin_ready, 1)
            for kind, g in ("g0", "g1", "g2", "g3", "d0", "d1", "g4", "d2", "g5", "d3", "g6", "d4", "g7", "d5", "d6", "d7"):
                (gate_half if kind == "g" else diagonals)(int(g))
            split_hi(fixed(N_OUT))
            split_hi(fixed(N_OUT + 1))

            act.wait_ge(total, before(BATCHES, S_MU + 1))
            act.wait_ge(rstd_ready, inverses(S_H0))
            load_root_table()
            act.activation(root[:, :], ps[:, sum_bank[S_MU], 0:T], ACT.Copy, scale=1.0 / D).then_inc(root_ready, 1)
            for q in range(4):
                square(S_VAR, q, quarter(y, q), centred, q + 1)
            take_root(S_VAR, D)
            for q in range(4):
                act.wait_ge(scaled, q + 1)
                for t in range(4 * q, 4 * q + 4):
                    last = act.activation(y[:, t, :], y[:, t, :], ACT.Silu, bias=cols[:, C_LNB + t:C_LNB + t + 1],
                                          scale=cols[:, C_LNG + t:C_LNG + t + 1])
                last.then_inc(silu_done, 1)
                act.wait_ge(silu_done, q + 1)
                act.activation(hid[:, 4 * q:4 * q + 4, 0, :], quarter(y, q), ACT.Copy).then_inc(xhi, 1)

            load_root_table()
            for k in range(4):
                group("out", fixed(G_OUT + k), fixed(N_OUT + GP * k), None, 0, None, None, k)

            def post_and_pre(ky, kh, r, outs):
                take_root(ky, D)
                if kh is None:
                    return
                for q in range(4):
                    square(kh, q, quarter(h, q), h_ready, 4 * r + q + 1)
                take_root(kh, D)
                for dst, cb_, i in outs:
                    shifted(dst, cb_, i)

            post_and_pre(S_Y0, S_H1, 0, [(xn, co_b, 0)])
            mlp(act, group, G_MLP0, N_MLP0, A_M0, A_UP, A_DOWN, A_UP + 1, 0)
            post_and_pre(S_Y1, S_H2, 1, [(hid, co_b2, 4)])
            split_hi(fixed(N_DQ + 2))
            split_hi(fixed(N_DQ + 3))
            shifted(xn, co_b, 8)
            split_hi(fixed(N_DQ + 4))
            split_hi(fixed(N_DQ + 5))
            halves(fixed(G_DQ), fixed(N_DQ), banks_of(G_DQ))

            def rank_square(k, i, at):
                act.wait_ge(evac_done, at)
                wait(act, total, before(BATCHES, k))
                act.activation(s3[:, :, :], quarter(y, 2 * i), ACT.Square).then_inc(squares, 1)

            def rank_high(i, dst):
                act.wait_ge(xf_ready, 12 + i + 1)
                act.activation(dst[:, :, 0, :], quarter(y, 2 * i), ACT.Copy).then_inc(xhi, 1)

            split_hi(fixed(N_KR + 2))
            rank_square(S_CQ, 0, G_DQ + 1)
            halves(fixed(G_KR), fixed(N_KR), banks_of(G_KR), 1, 1)
            split_hi(fixed(N_DKV + 2))
            take_root(S_CQ, RANK)
            rank_high(0, cq)
            for k in (3, 4, 5):
                split_hi(fixed(N_DKV + k))
            halves(fixed(G_DKV), fixed(N_DKV), banks_of(G_DKV))
            rank_square(S_CKV, 1, G_DKV + 1)
            take_root(S_CKV, RANK)
            rank_high(1, ckv)

            def evac_q(p):
                act.wait_ge(split_used, value(p, 0, 4) + 2 * (N_PAIR - N_OUT + 1))
                act.wait_ge(x_ready, 18)
                wait(act, scores, value(p))
                act.activation(qn, ps[:, 2, :].rearrange("p (j n) -> p j n", j=2), ACT.Copy).then_inc(q_copied, 1)

            def evac_kv(p):
                b = p.static % 2
                act.wait_ge(split_used, value(p, 1, 4) + 2 * (N_PAIR - N_OUT))
                wait(act, scores, value(p))
                act.activation(kn, ps[:, 0, :].rearrange("p (j n) -> p j n", j=2), ACT.Copy)
                wait(act, o_done, value(p, -1))
                act.activation(vv[:, b], ps[:, 1, :].rearrange("p (j n) -> p j n", j=2), ACT.Copy).then_inc(kv_copied, 1)

            def pair(p, n, more):
                split_hi(ahead(n, 3))
                act.wait_ge(maxed, value(p, 1, 2))
                for j in range(2):
                    for t in range(2):
                        lo, hi = (0, P) if t == 0 else (P, 3 * P)
                        last = act.activation(pr[:, j, lo:hi], pr[:, j, lo:hi], ACT.Exp, bias=stat[:, 0, j, t:t + 1],
                                              scale=SCALE, accum_out=stat[:, 1, j, t:t + 1])
                last.then_inc(exps, 1)
                act.wait_ge(sums_inverted, value(p, 1))
                for j in range(2):
                    for t in range(2):
                        lo, hi = (0, P) if t == 0 else (P, 3 * P)
                        last = act.activation(pr[:, j, lo:hi], pr[:, j, lo:hi], ACT.Copy, scale=stat[:, 2, j, t:t + 1])
                last.then_inc(probs_ready, 1)
                if more:
                    evac_q(ahead(p, 1))
                act.wait_ge(turned, value(p, 1))
                wait(act, o_done, value(p))
                act.activation(prt, ps[:, 6:8, 0:3 * P], ACT.Copy).then_inc(prt_ready, 1)
                if more:
                    split_hi(ahead(n, 4))
                    evac_kv(ahead(p, 1))
                act.wait_ge(o_done, value(p, 1))
                act.activation(hid[:, bass.ds(value(p, 0, 2), 2), 0, :], ps[:, 2, :].rearrange("p (j n) -> p j n", j=2), ACT.Copy).then_inc(o_hi, 1)

            evac_q(fixed(0))
            split_hi(fixed(N_PAIR + 2))
            evac_kv(fixed(0))
            looped(act, 3, lambda i: [pair(at_loop(k, (2, i)), at_loop(N_PAIR + 2 * k, (4, i)), True) for k in range(2)])
            pair(fixed(6), fixed(N_PAIR + 12), True)
            pair(fixed(7), fixed(N_PAIR + 14), False)

            load_root_table()
            for k in range(4):
                group("wo", fixed(G_WO + k), fixed(N_WO + GP * k), None, 0, None, None, k)
            post_and_pre(S_Y2, S_H3, 2, [(xn, co_b, 14)])
            mlp(act, group, G_MLP1, N_MLP1, A_M1, 1, 0, 1, 16)
            post_and_pre(S_Y3, None, 3, [])

        @block.vector
        def _(ve):
            steps = [0]

            def step(ins):
                steps[0] += 1
                ins.then_inc(step_done, 1)

            def settled():
                ve.wait_ge(step_done, steps[0])

            def split_lo(p):
                s, d = p.static % 4, p.static % 2
                for half in range(2):
                    at = slice(half * PIECE // 2, (half + 1) * PIECE // 2)
                    ve.wait_ge(hi_ready, value(p, -N_OUT, 2) + half + 1)
                    ve.tensor_tensor(wsp[:, d, 1, at], raw[:, s, at], wsp[:, d, 0, at].bitcast(f32), ALU.subtract).then_inc(lo_ready, 1)

            def mod_column(a):
                if not a.loops:
                    return mod[:, a.static:a.static + 1]
                return mod_step[:, a.static % 8:a.static % 8 + 1]

            def keep_mod(a, per):
                if a.loops and per:
                    ve.wait_ge(ada_used, value(a, per))
                    for k in range(per):
                        c0 = (a.static + k) % 8
                        last = ve.tensor_copy(mod[:, bass.ds(value(a, k), 1)], mod_step[:, c0:c0 + 1])
                    last.then_inc(mod_kept, 1)

            def reduce_ada(a):
                s = a.static % 2
                ve.wait_ge(ada_loaded[s], value(turn(ahead(a, -4), 2), 1, 16))
                ve.tensor_tensor_reduce(out=ada[:, s, :], in0=ada[:, s, :], in1=cb[:, :], scale=1.0, scalar=0.0,
                                        op0=ALU.mult, op1=ALU.add, accum_out=mod_column(a)).then_inc(ada_used, 1)

            def add_halves(g, b):
                ve.wait_ge(low_copied, value(g, 1))
                wait(ve, evac_done, value(g))
                ve.tensor_tensor(s0[:, :, :], ps[:, b:b + 4, 0:T], s1[:, :, :], ALU.add).then_inc(summed, 1)
                ve.wait_ge(summed, value(g, 1))

            def sum_quarter(k, q):
                ve.wait_ge(squares, before(SQUARES, k) + q + 1)
                ve.tensor_reduce(s2[:, q, :], s3[:, :, :].rearrange("p t n -> p n t"), AX.X, ALU.add).then_inc(partial, 1)

            def group(kind, g, n, a, per, t, u, q):
                order = group_order(GP, per)
                if q == 0:
                    gate_gain(LAST_OF[g.static + 4])
                if q:
                    run_order(order[:2], n, a, split_lo, reduce_ada)
                    sum_quarter(LAST_OF[g.static - q + 4], q - 1)
                    order = order[2:]
                late = order[-1:] if q == 3 else []
                run_order(order[:len(order) - len(late)], n, a, split_lo, reduce_ada)
                keep_mod(a, per)
                add_halves(g, 4 * (g.static % 2))
                at = bass.ds(value(t, 0, 4), 4)
                if kind == "out":
                    bias = cols[:, C_BOUT + 4 * q:C_BOUT + 4 * q + 4].rearrange("p (t o) -> p t o", o=1).broadcast_to([P, 4, T])
                    ve.tensor_tensor(quarter(y, q), s0[:, :, :], bias, ALU.add).then_inc(evac_done, 1)
                elif kind == "wo":
                    ve.tensor_copy(quarter(y, q), s0[:, :, :]).then_inc(evac_done, 1)
                elif kind == "down":
                    ve.wait_ge(y_cleared, 1 if g.static < G_DQ else 2)
                    ve.tensor_tensor(y[:, at, :], y[:, at, :], s0[:, :, :], ALU.add).then_inc(evac_done, 1)
                if kind != "up":
                    run_order(late, n, a, split_lo, reduce_ada)
                    return
                done = value(u) + value(t)
                ve.scalar_tensor_tensor(s2[:, :, :], s0[:, :, :], 0.0, s0[:, :, :], ALU.max, ALU.mult).then_inc(evac_done, 1)
                ve.wait_ge(hid_hi, done + 1)
                ve.tensor_tensor(hid[:, at, 1, :], s2[:, :, :], hid[:, at, 0, :].bitcast(f32), ALU.subtract).then_inc(hid_ready, 1)
                ve.wait_ge(hid_ready, done + 1)

            def quarter(buf, q):
                return buf[:, 4 * q:4 * q + 4, :]

            def invert(k):
                ve.wait_ge(root_ready, k + 1)
                ve.reciprocal(rstd[:, :], root[:, :]).then_inc(rstd_ready, 1)
                ve.wait_ge(rstd_ready, inverses(k))

            def wide(row, n=4):
                return row[:, :].rearrange("p (o n) -> p o n", o=1).broadcast_to([P, n, T])

            def scale_shift(ca, cb_, m, gain):
                step(ve.tensor_tensor(cb_[:, :], mod[:, m:m + NT], cols[:, C_BADA + m:C_BADA + m + NT], ALU.add))
                step(ve.tensor_tensor(ca[:, :], mod[:, m + NT:m + 2 * NT], cols[:, C_BADA + m + NT:C_BADA + m + 2 * NT], ALU.add))
                settled()
                step(ve.scalar_tensor_tensor(ca[:, :], ca[:, :], 1.0, cols[:, gain:gain + NT], ALU.add, ALU.mult))
                settled()

            def gate_gain(k):
                m, gain, used, kept = {
                    S_Y0: (M_MIX0 + 32, C_POSTMIX, A_OUT, 0), S_Y1: (M_MLP0 + 32, C_POSTMLP, A_M0 + 16, 28),
                    S_Y2: (M_MIX1 + 32, C_POSTMIX + NT, A_WO, 32), S_Y3: (M_MLP1 + 32, C_POSTMLP + NT, M_ALL, 48)}[k]
                ve.wait_ge(ada_used, used)
                wait(ve, mod_kept, kept)
                step(ve.tensor_tensor(co_g[:, :], mod[:, m:m + NT], cols[:, C_BADA + m:C_BADA + m + NT], ALU.add))
                settled()
                ve.tensor_tensor(co_g[:, :], co_g[:, :], cols[:, gain:gain + NT], ALU.mult).then_inc(gates_ready, 1)

            def times_gain(ca, r):
                wait(ve, h_ready, 4 * r)
                for t in range(NT):
                    last = ve.tensor_scalar(y[:, t, :], h[:, t, :], ca[:, t:t + 1], None, ALU.mult)
                step(last)

            def modulated(k, dst, cb_, i):
                settled()

                def times(q):
                    ve.tensor_tensor(quarter(y, q), quarter(y, q), wide(rstd), ALU.mult).then_inc(xf_ready, 1)
                times(0)
                for q in range(4):
                    if q < 3:
                        times(q + 1)
                    ve.wait_ge(xhi, i + q + 1)
                    for t in range(4 * q, 4 * q + 4):
                        last = ve.scalar_tensor_tensor(dst[:, t, 1, :], y[:, t, :], cb_[:, t:t + 1], dst[:, t, 0, :].bitcast(f32),
                                                       ALU.add, ALU.subtract)
                    last.then_inc(x_ready, 1)

            def residual(k, r):
                invert(k)

                def times(q):
                    ve.wait_ge(y_scaled, 4 * r + q + 1)
                    step(ve.tensor_tensor(quarter(y, q), quarter(y, q), wide(rstd), ALU.mult))
                times(0)
                for q in range(4):
                    at = steps[0]
                    if q < 3:
                        times(q + 1)
                    ve.wait_ge(step_done, at)
                    ve.tensor_tensor(quarter(h, q), quarter(h, q), quarter(y, q), ALU.add).then_inc(h_ready, 1)

            ve.memset(epsc[:, 0:1], EPS)
            ve.memset(epsc[:, 1:2], float(np.pi / 2))
            ve.memset(ones[:, :], 1.0)
            step(ve.memset(ubuf[:, :, :], 0.0))
            ve.wait_ge(small_loaded, 48)
            step(ve.tensor_copy(rstd[:, :], posi[:, :]))
            settled()
            step(ve.tensor_scalar(rstd[:, :], rstd[:, :], consts[:, K_INV:K_INV + 1], None, ALU.mult))
            settled()
            magic = 1.5 * 2.0 ** 23
            step(ve.tensor_scalar(root[:, :], rstd[:, :], float(1 / (2 * np.pi)), magic, ALU.mult, ALU.add))
            settled()
            step(ve.tensor_scalar(root[:, :], root[:, :], magic, None, ALU.subtract))
            settled()
            part1 = 6.28125
            part2 = float(np.float32(np.round((2 * np.pi - part1) * 2 ** 22) / 2 ** 22))
            part3 = float(2 * np.pi - part1 - part2)
            for part in (part1, part2, part3):
                step(ve.scalar_tensor_tensor(rstd[:, :], root[:, :], -part, rstd[:, :], ALU.mult, ALU.add))
                settled()
            below = float(np.nextafter(np.float32(np.pi), np.float32(0)))
            ve.tensor_scalar(rstd[:, :], rstd[:, :], below, -below, ALU.min, ALU.max).then_inc(ang, 1)
            ve.wait_ge(ang, 1)
            ve.scalar_tensor_tensor(root[:, :], rstd[:, :], -1.0, rstd[:, :], ALU.mult, ALU.max).then_inc(ang, 1)

            ve.wait_ge(c_ready, 1)
            for q in range(4):
                for a in range(8 * q, 8 * q + 8):
                    m = M_MIX0 + 4 * q + a % 4 + (NT if a % 8 >= 4 else 0)
                    if 2 <= a < 6:
                        buf = raw[:, a - 2, :]
                        ve.wait_ge(w_loaded[a - 2], 16)
                    else:
                        buf = ada[:, a % 2, :]
                        ve.wait_ge(ada_loaded[a % 2], 16 if a < 2 else 16 * ((a - 4) // 2 + 1))
                    ve.tensor_tensor_reduce(out=buf, in0=buf, in1=cb[:, :], scale=1.0, scalar=0.0,
                                            op0=ALU.mult, op1=ALU.add, accum_out=mod[:, m:m + 1]).then_inc(ada_used, 1)
                if q == 0:
                    invert(S_H0)
                    for k in range(4):
                        ve.tensor_tensor(quarter(y, k), quarter(h, k), wide(rstd), ALU.mult).then_inc(start_normed, 1)
                ve.wait_ge(ada_used, 8 * q + 8)
                at = slice(4 * q, 4 * q + 4)
                shift, scale = slice(M_MIX0 + 4 * q, M_MIX0 + 4 * q + 4), slice(M_MIX0 + NT + 4 * q, M_MIX0 + NT + 4 * q + 4)
                step(ve.tensor_tensor(co_b[:, at], mod[:, shift], cols[:, shift], ALU.add))
                step(ve.tensor_tensor(co_a[:, at], mod[:, scale], cols[:, scale], ALU.add))
                settled()
                ve.scalar_tensor_tensor(co_a[:, at], co_a[:, at], 1.0, cols[:, C_PREMIX + 4 * q:C_PREMIX + 4 * q + 4],
                                        ALU.add, ALU.mult).then_inc(coef_ready, 1)

            def accumulator(g):
                return (s2, s0)[g // 2 % 2][:, 2 * (g % 2):2 * (g % 2) + 2, :]

            OWN = 2 * (WIDTH - PE_TAPS)

            def gated(g):
                ve.wait_ge(sig_ready, g + 1)
                wait(ve, taps, OWN * (g - 3))
                wait(ve, pe_taps, g - 3)
                for t in range(2):
                    c0 = C_CONV + CONV * g + t
                    last = ve.scalar_tensor_tensor(ubuf[:, g % 4, t, WIDTH - 1:], ps[:, in_bank(g), T * t:T * t + T], cols[:, c0:c0 + 1],
                                                   s1[:, 2 * (g % 2) + t, :], ALU.add, ALU.mult)
                last.then_inc(u_ready, 1)

            def finish_conv(g):
                ve.wait_ge(taps, OWN * (g + 1))
                ve.wait_ge(pe_taps, g + 1)
                ve.tensor_tensor(y[:, 2 * g:2 * g + 2, :], accumulator(g),
                                 ps[:, TAP_BANKS[g], :].rearrange("p (t n) -> p t n", t=2), ALU.add).then_inc(conv_done, 1)

            def add_taps(g):
                for k in range(A_CONV // 2):
                    reduce_ada(fixed(A_IN + A_CONV * g + k))
                if g >= 4:
                    finish_conv(g - 4)
                    ve.wait_ge(conv_done, g - 3)
                ve.wait_ge(u_ready, g + 1)
                for w in range(PE_TAPS, WIDTH):
                    if w == (PE_TAPS + WIDTH) // 2:
                        for k in range(A_CONV // 2, A_CONV):
                            reduce_ada(fixed(A_IN + A_CONV * g + k))
                    for t in range(2):
                        acc, u = accumulator(g)[:, t, :], ubuf[:, g % 4, t, w:w + T]
                        c0 = C_CONV + CONV * g + GT + t * (WIDTH + 1)
                        if w == PE_TAPS:
                            ve.tensor_scalar(acc, u, cols[:, c0 + w:c0 + w + 1], cols[:, c0 + WIDTH:c0 + WIDTH + 1],
                                             ALU.mult, ALU.add).then_inc(taps, 1)
                            continue
                        ve.wait_ge(taps, OWN * g + 2 * (w - PE_TAPS - 1) + t + 1)
                        ve.scalar_tensor_tensor(acc, u, cols[:, c0 + w:c0 + w + 1], acc, ALU.mult, ALU.add).then_inc(taps, 1)

            for kind, g in ("g0", "g1", "g2", "g3", "t0", "g4", "t1", "t2", "t3", "g5", "t4", "g6", "t5", "g7", "t6", "t7"):
                (gated if kind == "g" else add_taps)(int(g))
            split_lo(fixed(N_OUT))
            for g in range(IN_GROUPS - 4, IN_GROUPS):
                finish_conv(g)
            split_lo(fixed(N_OUT + 1))

            reduce_ada(fixed(A_LN))
            ve.wait_ge(conv_done, IN_GROUPS)
            ve.wait_ge(root_ready, S_MU + 1)
            for q in range(4):
                ve.tensor_tensor(quarter(y, q), quarter(y, q), wide(root), ALU.subtract).then_inc(centred, 1)
            reduce_ada(fixed(A_LN + 1))
            reduce_ada(fixed(A_LN + 2))
            invert(S_VAR)
            for q in range(4):
                ve.tensor_tensor(quarter(y, q), quarter(y, q), wide(rstd), ALU.mult).then_inc(scaled, 1)
            for q in range(4):
                ve.wait_ge(xhi, q + 1)
                ve.tensor_tensor(hid[:, 4 * q:4 * q + 4, 1, :], quarter(y, q), hid[:, 4 * q:4 * q + 4, 0, :].bitcast(f32),
                                 ALU.subtract).then_inc(x_ready, 1)

            reduce_ada(fixed(A_LN + 3))
            for k in range(4):
                group("out", fixed(G_OUT + k), fixed(N_OUT + GP * k), fixed(A_OUT + A_OUT_GROUP * k), A_OUT_GROUP, fixed(k), None, k)

            ve.wait_ge(evac_done, G_MLP0)
            ve.wait_ge(ada_used, A_M0)
            scale_shift(co_a, co_b, M_MLP0, C_PREMLP)
            residual(S_Y0, 0)
            times_gain(co_a, 1)
            invert(S_H1)
            modulated(S_H1, xn, co_b, 4)
            ve.wait_ge(x_ready, 8)
            mlp(ve, group, G_MLP0, N_MLP0, A_M0, A_UP, A_DOWN, A_UP + 1, 0)

            ve.wait_ge(evac_done, G_DQ)
            ve.wait_ge(ada_used, A_DKV)
            scale_shift(co_a2, co_b2, M_MIX1, C_PREMIX + NT)
            scale_shift(co_a, co_b, M_KV, C_GKV)
            residual(S_Y1, 1)
            times_gain(co_a2, 2)
            invert(S_H2)
            modulated(S_H2, hid, co_b2, 8)
            split_lo(fixed(N_DQ + 2))
            ve.wait_ge(x_ready, 12)
            times_gain(co_a, 2)
            split_lo(fixed(N_DQ + 3))
            modulated(S_H2, xn, co_b, 12)
            split_lo(fixed(N_DQ + 4))
            split_lo(fixed(N_DQ + 5))

            def rank_sum(g, i):
                add_halves(fixed(g), banks_of(g))
                ve.wait_ge(x_ready, 16)
                ve.tensor_copy(quarter(y, 2 * i), s0[:, :, :]).then_inc(evac_done, 1)

            def rank_norm(k, i, gain, dst):
                invert(k)
                step(ve.tensor_tensor(quarter(y, 2 * i), quarter(y, 2 * i), wide(rstd), ALU.mult))
                settled()
                for t in range(RT):
                    last = ve.tensor_scalar(y[:, 8 * i + t, :], y[:, 8 * i + t, :], cols[:, gain + t:gain + t + 1], None, ALU.mult)
                last.then_inc(xf_ready, 1)
                ve.wait_ge(xhi, 16 + i + 1)
                ve.tensor_tensor(dst[:, :, 1, :], quarter(y, 2 * i), dst[:, :, 0, :].bitcast(f32), ALU.subtract).then_inc(x_ready, 1)

            rank_sum(G_DQ, 0)
            split_lo(fixed(N_KR + 2))
            b = banks_of(G_KR)
            ve.wait_ge(low_copied, G_KR + 1)
            ve.wait_ge(evac_done, G_KR)
            ve.tensor_tensor(s0[:, 0, :], ps[:, b, 0:T], s1[:, 0, :], ALU.add).then_inc(summed, 1)
            ve.wait_ge(summed, G_KR + 1)
            step(ve.tensor_tensor(s2[0:ROPE, 0, :], s0[0:ROPE, 0, :], table[0:ROPE, :], ALU.mult))
            step(ve.tensor_tensor(s2[0:ROPE, 1, :], s0[ROPE:P, 0, :], table[ROPE:P, :], ALU.mult))
            settled()
            ve.tensor_tensor(krope[:, :], s2[0:ROPE, 0, :], s2[0:ROPE, 1, :], ALU.add).then_inc(evac_done, 1)
            split_lo(fixed(N_DKV + 2))
            rank_norm(S_CQ, 0, C_GCQ, cq)
            reduce_ada(fixed(A_DKV))
            reduce_ada(fixed(A_DKV + 1))
            split_lo(fixed(N_DKV + 3))
            reduce_ada(fixed(A_DKV + 2))
            reduce_ada(fixed(A_DKV + 3))
            split_lo(fixed(N_DKV + 4))
            split_lo(fixed(N_DKV + 5))
            rank_sum(G_DKV, 1)
            rank_norm(S_CKV, 1, C_GCKV, ckv)

            def rotate_q(p):
                ve.wait_ge(split_used, value(p, 0, 4) + 2 * (N_PAIR - N_OUT + 1))
                wait(ve, scores, value(p))
                tab = table[:, :].rearrange("p (o n) -> p o n", o=1).broadcast_to([P, 2, T])
                both = ps[:, 3, :].rearrange("p (j n) -> p j n", j=2)
                wait(ve, q_ready, value(p))
                ve.tensor_tensor(s2[0:ROPE, 0:2, :], both[0:ROPE], tab[0:ROPE], ALU.mult).then_inc(q_step, 1)
                ve.tensor_tensor(s2[0:ROPE, 2:4, :], both[ROPE:P], tab[ROPE:P], ALU.mult).then_inc(q_step, 1)
                ve.wait_ge(q_step, value(p, 1, 2))
                ve.tensor_tensor(qr, s2[0:ROPE, 0:2, :], s2[0:ROPE, 2:4, :], ALU.add).then_inc(q_ready, 1)

            def pair(p, n, a, more):
                ve.wait_ge(scores, value(p, 1))
                wait(ve, turned, value(p))
                ve.tensor_tensor(pr, ps[:, 4:6, 0:3 * P], mask.broadcast_to([P, 2, 3 * P]), ALU.add).then_inc(masked, 1)
                ve.wait_ge(masked, value(p, 1))
                ve.tensor_reduce(stat[:, 0, :, 0], pr[:, :, 0:P], AX.X, ALU.max)
                ve.tensor_reduce(stat[:, 0, :, 1], pr[:, :, P:3 * P], AX.X, ALU.max).then_inc(maxed, 1)
                ve.wait_ge(maxed, value(p, 0, 2) + 1)
                ve.tensor_scalar(stat[:, 0, :, :], stat[:, 0, :, :], -SCALE, None, ALU.mult).then_inc(maxed, 1)
                split_lo(ahead(n, 3))
                ve.wait_ge(exps, value(p, 1))
                ve.reciprocal(stat[:, 2, :, :], stat[:, 1, :, :]).then_inc(sums_inverted, 1)
                if more:
                    rotate_q(ahead(p, 1))
                reduce_ada(a)
                if more:
                    split_lo(ahead(n, 4))
                reduce_ada(ahead(a, 1))
                ve.wait_ge(o_hi, value(p, 1))
                at = bass.ds(value(p, 0, 2), 2)
                ve.tensor_tensor(hid[:, at, 1, :], ps[:, 2, :].rearrange("p (j n) -> p j n", j=2), hid[:, at, 0, :].bitcast(f32),
                                 ALU.subtract).then_inc(o_ready, 1)
                for k in range(2, A_PER_PAIR):
                    reduce_ada(ahead(a, k))
                keep_mod(a, A_PER_PAIR)

            rotate_q(fixed(0))
            split_lo(fixed(N_PAIR + 2))
            looped(ve, 3, lambda i: [pair(at_loop(k, (2, i)), at_loop(N_PAIR + 2 * k, (4, i)), at_loop(A_PAIR + A_PER_PAIR * k, (2 * A_PER_PAIR, i)), True)
                                     for k in range(2)])
            pair(fixed(6), fixed(N_PAIR + 12), fixed(A_PAIR + 6 * A_PER_PAIR), True)
            pair(fixed(7), fixed(N_PAIR + 14), fixed(A_PAIR + 7 * A_PER_PAIR), False)

            for k in range(4):
                group("wo", fixed(G_WO + k), fixed(N_WO + GP * k), fixed(A_WO + A_WO_GROUP * k), A_WO_GROUP, fixed(k), None, k)

            ve.wait_ge(evac_done, G_MLP1)
            ve.wait_ge(ada_used, A_M1)
            ve.wait_ge(mod_kept, 32)
            scale_shift(co_a, co_b, M_MLP1, C_PREMLP + NT)
            residual(S_Y2, 2)
            times_gain(co_a, 3)
            invert(S_H3)
            modulated(S_H3, xn, co_b, 18)
            ve.wait_ge(x_ready, 22)
            mlp(ve, group, G_MLP1, N_MLP1, A_M1, 1, 0, 1, 16)
            ve.wait_ge(evac_done, G_MLP1 + 8 * CHUNKS)
            residual(S_Y3, 3)

        @block.gpsimd
        def _(pool):
            for at in (8, 22):
                pool.wait_ge(x_ready, at)
                pool.memset(y[:, :, :], 0.0).then_inc(y_cleared, 1)

        @block.tensor
        def _(pe):
            def product(g, n, src, ready, at, between=None):
                b = 4 * (g.static % 2)
                wait(pe, summed, value(g, -1))
                for j in range(GP):
                    if between and j in between:
                        between[j]()
                    if ready is not None:
                        pe.wait_ge(ready, at + j + 1)
                    d = (n.static + j) % 2
                    for k in range(4):
                        if k % 2 == 0:
                            pe.wait_ge(lo_ready, value(n, j - N_OUT, 2) + k // 2 + 1)
                        for o in range(GT):
                            at_w = slice((k * GT + o) * P, (k * GT + o + 1) * P)
                            kt = 4 * j + k
                            first, end = kt == 0, kt == NT - 1

                            def high():
                                return pe.matmul(ps[:, b + o, :], wsp[:, d, 0, at_w], src[:, kt, :, :].rearrange("p a n -> p (a n)"), start=first, stop=end)

                            def low():
                                return pe.matmul(ps[:, b + o, 0:T], wsp[:, d, 1, at_w], src[:, kt, 0, :], start=False, stop=False)
                            if first:
                                high()
                                last = low()
                            else:
                                low()
                                last = high()
                        if k % 2:
                            last.then_inc(split_used, 1)

            def over_partitions(k, src, first, end):
                return pe.matmul(ps[:, sum_bank[k], 0:T], ones[:, :], src, start=first, stop=end)

            def keep_warm(bank, n):
                for _ in range(n):
                    pe.matmul(ps[:, bank, :], ones[:, :], consts[:, K_IDENT:K_IDENT + 4 * P], start=True, stop=True)

            def sum_partials(k, g):
                pe.wait_ge(summed, g)
                pe.wait_ge(partial, before(PARTIALS, k + 1))
                for q in range(3):
                    over_partitions(k, s2[:, q, :], q == 0, False)

            def sum_y(k):
                keep_warm(sum_bank[k] + 1, 7)
                pe.wait_ge(squares, before(SQUARES, k + 1))
                for t in range(4):
                    last = over_partitions(k, s3[:, t, :], False, t == 3)
                last.then_inc(total, 1)

            def sum_quarters(k, warm=None):
                if warm:
                    keep_warm(warm, 5)
                for q in range(SQUARES[k]):
                    pe.wait_ge(squares, before(SQUARES, k) + q + 1)
                    for t in range(4):
                        last = over_partitions(k, (s3, s0)[q % 2][:, t, :], q + t == 0, q == SQUARES[k] - 1 and t == 3)
                    last.then_inc(total, 1)
                if warm:
                    keep_warm(warm, 6)

            def with_partials(g, q):
                return {3: lambda: sum_partials(LAST_OF[g.static + 1], g.static)} if q == 3 else None

            def group(kind, g, n, a, per, t, u, q):
                if kind == "up":
                    product(g, n, xn, x_ready, 4 if g.static < G_DQ else 18)
                else:
                    product(g, n, hid, hid_ready, value(u), with_partials(g, q))

            pe.wait_ge(step_done, 1)
            pe.wait_ge(small_loaded, 48)
            sum_quarters(S_H0)

            def unsplit(g, n, j):
                s = n % 4
                pe.wait_ge(w_loaded[s], 16 * (n // 4 + 2))
                for k in range(4):
                    for o in range(GT):
                        kt, at_w = 4 * j + k, slice((k * GT + o) * P, (k * GT + o + 1) * P)
                        last = pe.matmul(ps[:, in_bank(g) + o // 2, T * (o % 2):T * (o % 2) + T], raw[:, s, at_w], xf[:, kt, :],
                                         start=kt == 0 and o % 2 == 0, stop=kt == NT - 1 and o % 2 == 1, skip_group_check=True)
                last.then_inc(native_used, 1)

            for j in range(GP):
                pe.wait_ge(xin_ready, j + 1)
                for g in range(START_GROUPS):
                    if g == 3 and j == 0:
                        pe.wait_ge(start_normed, 4)
                    unsplit(g, 4 * j + g, j)

            def in_product(g):
                pe.wait_ge(u_ready, {4: 1, 5: 2, 6: 5, 7: 6}[g])
                for j in range(GP):
                    unsplit(g, GP * g + j, j)

            def add_taps(g):
                pe.wait_ge(diag_ready, g + 1)
                pe.wait_ge(u_ready, max(g + 1, START_GROUPS))
                if g < 6:
                    wait(pe, conv_done, g - 2)
                for t in range(2):
                    for w in range(PE_TAPS):
                        last = pe.matmul(ps[:, TAP_BANKS[g], T * t:T * t + T], diag[g % 2][:, t, w, :], ubuf[:, g % 4, t, w:w + T],
                                         start=w == 0, stop=w == PE_TAPS - 1)
                last.then_inc(pe_taps, 1)

            def add_mean(g):
                pe.wait_ge(conv_done, g + 1)
                for t in range(2):
                    last = over_partitions(S_MU, y[:, 2 * g + t, :], g + t == 0, g == IN_GROUPS - 1 and t == 1)
                if g == IN_GROUPS - 1:
                    last.then_inc(total, 1)

            for kind, g in ("p4", "t0", "p5", "t1", "p6", "t2", "p7", "t3", "t4", "t5", "m0", "t6", "m1", "m2", "t7",
                            "m3", "m4", "m5", "m6", "m7"):
                {"p": in_product, "t": add_taps, "m": add_mean}[kind](int(g))
            sum_quarters(S_VAR, 5)

            for k in range(4):
                product(fixed(G_OUT + k), fixed(N_OUT + GP * k), hid, x_ready, 0, with_partials(fixed(G_OUT + k), k))
            sum_y(S_Y0)
            sum_quarters(S_H1, sum_bank[S_Y0] + 1)
            mlp(pe, group, G_MLP0, N_MLP0, A_M0, A_UP, A_DOWN, A_UP + 1, 0)
            sum_y(S_Y1)
            sum_quarters(S_H2, sum_bank[S_Y1] + 1)

            product(fixed(G_DQ), fixed(N_DQ), hid, x_ready, 8)
            b, d = banks_of(G_KR), N_KR % 2
            for kt in range(NT):
                if kt % 4 == 0:
                    pe.wait_ge(x_ready, 12 + kt // 4 + 1)
                if kt % 8 == 0:
                    pe.wait_ge(lo_ready, 2 * (N_KR - N_OUT) + kt // 8 + 1)
                at_w = slice(kt * P, (kt + 1) * P)
                if kt:
                    pe.matmul(ps[:, b, 0:T], wsp[:, d, 1, at_w], xn[:, kt, 0, :], start=False, stop=False)
                last = pe.matmul(ps[:, b, :], wsp[:, d, 0, at_w], xn[:, kt, :, :].rearrange("p a n -> p (a n)"), start=kt == 0, stop=kt == NT - 1)
                if not kt:
                    last = pe.matmul(ps[:, b, 0:T], wsp[:, d, 1, at_w], xn[:, kt, 0, :], start=False, stop=False)
                if kt % 8 == 7:
                    last.then_inc(split_used, 1)

            def sum_rank(k):
                pe.wait_ge(squares, before(SQUARES, k + 1))
                for t in range(RT):
                    last = over_partitions(k, s3[:, t, :], t == 0, t == RT - 1)
                last.then_inc(total, 1)

            product(fixed(G_DKV), fixed(N_DKV), xn, None, 0, {1: lambda: sum_rank(S_CQ)})

            def three(bank, at, d, w_at, src):
                last = None
                for kt in range(RT):
                    wa = slice(kt * 512 + w_at, kt * 512 + w_at + P)
                    for m, (wi, xi) in enumerate(((0, 0), (0, 1), (1, 0))):
                        before_last, last = last, pe.matmul(ps[:, bank, at:at + T], wsp[:, d, wi, wa], src[:, kt, xi, :],
                                                            start=kt == 0 and m == 0, stop=kt == RT - 1 and m == 2)
                return before_last, last

            def project_q(p, n):
                wait(pe, q_copied, value(p))
                wait(pe, q_ready, value(p))
                wait(pe, o_ready, value(p, -1))
                d = n.static % 2
                pe.wait_ge(lo_ready, value(n, 1 - N_OUT, 2))
                for j in range(2):
                    three(2, T * j, d, 2 * P * j, cq)
                for j in range(2):
                    before_last, last = three(3, T * j, d, 2 * P * j + P, cq)
                before_last.then_inc(split_used, 1)
                last.then_inc(split_used, 1)

            def project_kv(p, n):
                wait(pe, kv_copied, value(p))
                d = (n.static + 1) % 2
                pe.wait_ge(lo_ready, value(n, 2 - N_OUT, 2))
                for j in range(2):
                    three(0, T * j, d, P * j, ckv)
                last = None
                for tt in range(2):
                    for kt in range(RT):
                        wa = slice(kt * 512 + 2 * P, kt * 512 + 4 * P)
                        for m, (wi, xi) in enumerate(((0, 0), (0, 1), (1, 0))):
                            before_last, last = last, pe.matmul(ps[:, 1, T * tt:T * tt + T], ckv[:, kt, xi, P * tt:P * tt + P], wsp[:, d, wi, wa],
                                                                start=kt == 0 and m == 0, stop=kt == RT - 1 and m == 2)
                before_last.then_inc(split_used, 1)
                last.then_inc(split_used, 1)

            def score(p):
                pe.wait_ge(kv_copied, value(p, 1))
                pe.wait_ge(q_copied, value(p, 1))
                pe.wait_ge(q_ready, value(p, 1))
                wait(pe, masked, value(p))
                for j in range(2):
                    for t in range(2):
                        at, keys = (0, P) if t == 0 else (P, T)
                        pe.matmul(ps[:, 4 + j, at:at + keys], qn[:, j, P * t:P * t + P], kn[:, j, 0:keys], start=True, stop=False)
                        last = pe.matmul(ps[:, 4 + j, at:at + keys], qr[:, j, P * t:P * t + P], krope[:, 0:keys], start=False, stop=True)
                last.then_inc(scores, 1)

            def transpose(p):
                pe.wait_ge(probs_ready, value(p, 1))
                wait(pe, prt_ready, value(p))
                for j in range(2):
                    for k in range(3):
                        last = pe.transpose(ps[:, 6 + j, P * k:P * k + P], pr[:, j, P * k:P * k + P], ident)
                last.then_inc(turned, 1)

            def attend(p, more):
                b = p.static % 2
                pe.wait_ge(prt_ready, value(p, 1))
                if more:
                    pe.wait_ge(q_copied, value(p, 2))
                for j in range(2):
                    pe.matmul(ps[:, 2, T * j:T * j + T], vv[:, b, 0, P * j:P * j + P], prt[:, j, 0:T], start=True, stop=False)
                    last = pe.matmul(ps[:, 2, T * j + P:T * j + T], vv[:, b, 1, P * j:P * j + P], prt[:, j, T:T + P], start=False, stop=True)
                last.then_inc(o_done, 1)

            pe.wait_ge(x_ready, 17)
            pe.wait_ge(summed, G_DKV + 1)
            project_q(fixed(0), fixed(N_PAIR))
            sum_rank(S_CKV)
            pe.wait_ge(x_ready, 18)
            project_kv(fixed(0), fixed(N_PAIR))

            def pair(p, n, more):
                score(p)
                if more:
                    project_q(ahead(p, 1), ahead(n, 2))
                transpose(p)
                if more:
                    project_kv(ahead(p, 1), ahead(n, 2))
                attend(p, more)
            looped(pe, 3, lambda i: [pair(at_loop(k, (2, i)), at_loop(N_PAIR + 2 * k, (4, i)), True) for k in range(2)])
            pair(fixed(6), fixed(N_PAIR + 12), True)
            pair(fixed(7), None, False)

            pe.wait_ge(o_ready, HEADS // 2)

            for k in range(4):
                product(fixed(G_WO + k), fixed(N_WO + GP * k), hid, None, 0, with_partials(fixed(G_WO + k), k))
            sum_y(S_Y2)
            sum_quarters(S_H3, sum_bank[S_Y2] + 1)
            mlp(pe, group, G_MLP1, N_MLP1, A_M1, 1, 0, 1, 16)
            sum_y(S_Y3)


def _tiles(w):
    k, n = w.shape
    return w.reshape(k // P, P, n // P, P).transpose(0, 2, 1, 3)


def _group(w, tiles):
    t = _tiles(w)[:, tiles]
    kt = t.shape[0]
    return t.reshape(kt // 4, 4, 4, P, P).transpose(0, 3, 1, 2, 4).reshape(kt // 4, P, PIECE)


def _streams(a):
    w = []

    def groups(m):
        for n in range(m.shape[1] // (GT * P)):
            w.append(_group(m, list(range(GT * n, GT * n + GT))))

    def mlp(l):
        for ch in range(CHUNKS):
            groups(a["mlp_w_up"][l][:, ch * D:(ch + 1) * D])
            groups(a["mlp_w_down"][l][ch * D:(ch + 1) * D])
    conv = [_group(a["conv_w_in"][0], [2 * g, 2 * g + 1, NT + 2 * g, NT + 2 * g + 1]) for g in range(IN_GROUPS)]
    w.append(np.stack(conv[:START_GROUPS], axis=1).reshape(-1, P, PIECE))
    w += conv[START_GROUPS:]
    groups(a["conv_w_out"][0])
    mlp(0)
    groups(a["w_dq"][0])
    kr = a["w_kr"]
    kr = np.concatenate([kr, kr[:, ROPE // 2:], kr[:, :ROPE // 2]], axis=1)
    w.append(kr.reshape(NT, P, P).transpose(1, 0, 2).reshape(1, P, PIECE))
    groups(a["w_dkv"])
    uk = a["w_uk"].reshape(RT, P, HEADS // 2, 2 * NOPE)
    uv = a["w_uv"].reshape(RT, P, HEADS // 2, 2 * VDIM)
    kv = np.concatenate([uk, uv], axis=3).transpose(2, 1, 0, 3).reshape(HEADS // 2, 1, P, PIECE)
    uq = a["w_uq"][0].reshape(RT, P, HEADS // 2, 2, NOPE + ROPE)
    half = NOPE + ROPE // 2
    uq = np.concatenate([uq, uq[..., half:], uq[..., NOPE:half]], axis=4)
    uq = uq.transpose(2, 1, 0, 3, 4).reshape(HEADS // 2, 1, P, PIECE)
    w.append(np.concatenate([uq, kv], axis=1).reshape(HEADS, P, PIECE))
    groups(a["w_o"][0])
    mlp(1)
    ada = [a["w_ada_mix"][0], a["w_ada_mlp"][0], a["w_ada_kv"], a["w_ada_mix"][1], a["w_ada_mlp"][1]]
    ada = np.concatenate([m.T.reshape(-1, P, D) for m in ada])
    first = [at + 4 * q + k for q in range(4) for at in (0, NT) for k in range(4)]
    ada = np.concatenate([ada[first], ada[A_START:]])
    return np.concatenate(w), ada


def _columns(a):
    def col(v):
        return np.asarray(v).reshape(-1, P).T
    bada = [a["b_ada_mix"][0], a["b_ada_mlp"][0], a["b_ada_kv"], a["b_ada_mix"][1], a["b_ada_mlp"][1]]
    b_in = a["conv_b_in"][0].reshape(2, IN_GROUPS, 2, P).transpose(1, 0, 2, 3).reshape(IN_GROUPS, GT, P)
    dw = np.concatenate([a["conv_dw"][0], a["conv_dw_b"][0][None]]).reshape(WIDTH + 1, IN_GROUPS, 2, P)
    conv = np.concatenate([b_in, dw.transpose(1, 2, 0, 3).reshape(IN_GROUPS, 2 * (WIDTH + 1), P)], axis=1)
    parts = [*bada, a["g_pre_mix"], a["g_post_mix"], a["g_pre_mlp"], a["g_post_mlp"], conv,
             a["conv_ln_g"], a["conv_ln_b"], a["conv_b_out"], a["g_kv"], a["g_ckv"], a["g_cq"]]
    return np.ascontiguousarray(np.concatenate([col(v) for v in parts], axis=1))


def _constants():
    k = np.zeros((P, K_ALL), np.float32)
    inv = 1.0 / (np.float32(THETA) ** (np.arange(0, ROPE, 2, dtype=np.float32) / np.float32(ROPE)))
    k[:, K_INV] = np.tile(inv.astype(np.float32), 4)
    k[:, K_SIGN] = np.where(np.arange(P) % ROPE < ROPE // 2, -1.0, 1.0)
    k[:, K_IDENT:K_IDENT + P] = np.eye(P)
    tri = np.where(np.arange(P)[None, :] <= np.arange(P)[:, None], 0.0, NEG)
    k[:, K_MASK:K_MASK + P] = tri
    k[:, K_MASK + 2 * P:] = tri
    return k


def kernel(**inputs):
    import concourse.bacc as _bacc
    from concourse.bass_utils import run_bass_kernel_spmd as _run

    a = {k: np.asarray(v) for k, v in inputs.items()}
    w, ada = _streams(a)
    arrays = {
        "x_t": np.ascontiguousarray(a["x"][0].T.reshape(NT, P, T).transpose(1, 0, 2)),
        "c": a["c"][0],
        "positions": a["positions"][0],
        "columns": _columns(a),
        "constants": _constants(),
        "w_stream": w,
        "ada_stream": ada,
    }
    nc = _bacc.Bacc("TRN2", target_bir_lowering=False, num_devices=1, dynamic_dma_scratch_size=1024)
    args = [nc.dram_tensor(n, v.shape, mybir.dt.from_np(v.dtype), kind="ExternalInput").ap() for n, v in arrays.items()]
    out = nc.dram_tensor("out_t", (P, NT, T), mybir.dt.float32, kind="ExternalOutput").ap()
    trunk(nc, *args, out)
    r = _run(nc, [arrays], core_ids=[0])
    got = r.results[0]["out_t"]
    return np.ascontiguousarray(np.asarray(got).transpose(1, 0, 2).reshape(D, T).T)[None]
```

```python
from collections import namedtuple
from contextlib import ExitStack

import concourse.bass as bass
import numpy as np
from concourse import mybir

P = 128
D = 2048
T = 256
NT = D // P
WIDTH = 31
HEADS, NOPE, ROPE, VDIM, RANK = 16, 128, 64, 128, 512
RT = RANK // P
FF = 4 * D
CHUNKS = FF // D
THETA = 10000.0
EPS = 1e-6
SCALE = float(NOPE + ROPE) ** -0.5
NEG = -1e30
PIECE = 2048
GT = 4
GP = NT // 4

G_OUT, G_MLP0 = 0, 4
G_DQ = G_MLP0 + 2 * GT * CHUNKS
G_KR, G_DKV, G_WO = G_DQ + 1, G_DQ + 2, G_DQ + 3
G_MLP1 = G_WO + 4
N_IN, N_OUT, N_MLP0 = 0, 32, 48
N_DQ = N_MLP0 + 8 * GP * CHUNKS
N_KR = N_DQ + GP
N_DKV = N_KR + 1
N_PAIR = N_DKV + GP
N_WO = N_PAIR + HEADS
N_MLP1 = N_WO + 4 * GP
N_ALL = N_MLP1 + 8 * GP * CHUNKS

M_MIX0, M_MLP0, M_KV, M_MIX1, M_MLP1 = 0, 48, 96, 128, 176
M_ALL = 224
IN_GROUPS = 2 * NT // GT
START_GROUPS = 4
PE_TAPS = 12
A_START, A_CONV, A_UP, A_DOWN = 32, 4, 2, 3
A_IN, A_LN, A_OUT, A_M0 = 32, 64, 68, 80
A_OUT_GROUP = 3
A_DKV = A_M0 + GT * (CHUNKS * (A_UP + A_DOWN) + 1)
A_PAIR = A_DKV + 4
A_PER_PAIR, A_WO_GROUP = 3, 4
A_WO = A_PAIR + A_PER_PAIR * HEADS // 2
A_M1 = A_WO + 4 * A_WO_GROUP

C_BADA = 0
C_PREMIX, C_POSTMIX, C_PREMLP, C_POSTMLP = 224, 256, 288, 320
C_CONV = 352
CONV = GT + 2 * (WIDTH + 1)
C_LNG = C_CONV + IN_GROUPS * CONV
C_LNB, C_BOUT, C_GKV = C_LNG + 16, C_LNG + 32, C_LNG + 48
C_GCKV, C_GCQ = C_LNG + 64, C_LNG + 68
C_ALL = C_LNG + 72
K_INV, K_SIGN, K_IDENT, K_MASK = 0, 1, 2, 130
K_ALL = K_MASK + 3 * P

S_H0, S_MU, S_VAR, S_Y0, S_H1, S_Y1, S_H2, S_CQ, S_CKV, S_Y2, S_H3, S_Y3 = range(12)
SQUARES = [4, 0, 4, 4, 4, 4, 4, 1, 1, 4, 4, 4]
BATCHES = [4, 1, 4, 1, 4, 1, 4, 1, 1, 1, 4, 1]
PARTIALS = [0, 0, 0, 3, 0, 3, 0, 0, 0, 3, 0, 3]

Pos = namedtuple("Pos", "static loops")


def at_loop(n, *loops):
    return Pos(n, tuple(x for x in loops if x[1] is not None))


def fixed(n):
    return Pos(n, ())


def ahead(p, k):
    return Pos(p.static + k, p.loops)


def value(p, plus=0, times=1):
    n = times * (p.static + plus)
    for step, reg in p.loops:
        n = n + times * step * reg
    return n


def turn(p, ring):
    return Pos(p.static // ring, tuple((step // ring, reg) for step, reg in p.loops))


def wait(eng, sem, v):
    if not (isinstance(v, int) and v <= 0):
        eng.wait_ge(sem, v)


def trunk(nc, x_t, c, pos, cols_d, consts_d, w_stream, ada_stream, out_t):
    f32, f32r, i32 = mybir.dt.float32, mybir.dt.float32r, mybir.dt.int32
    ALU, ACT, AX = mybir.AluOpType, mybir.ActivationFunctionType, mybir.AxisListType
    ctx = ExitStack()
    with ctx:
        def sb(name, shape, dt=f32):
            return ctx.enter_context(nc.sbuf_tensor(name, shape, dt))

        def sem(name):
            return ctx.enter_context(nc.semaphore(name))

        h = sb("h", [P, NT, T])
        with (nc.sbuf_tensor("diag0", [P, 2, PE_TAPS, P], f32) as diag0, nc.sbuf_tensor("xn_end", [P, NT * T * 2 - 2 * PE_TAPS * P], f32),
              nc.sbuf_tensor("xf", [P, NT, T], f32) as xf, nc.sbuf_tensor("diag1", [P, 2, PE_TAPS, P], f32) as diag1):
            diag = (diag0, diag1)
        xn = sb("xn", [P, NT, 2, T], f32r)
        hid = sb("hid", [P, NT, 2, T], f32r)
        y = sb("y", [P, NT, T])
        raw = sb("raw", [P, 4, PIECE])
        wsp = sb("wsp", [P, 2, 2, PIECE], f32r)
        ada = sb("ada", [P, 2, PIECE])
        cb = sb("cb", [P, D])
        s0 = sb("s0", [P, 4, T])
        s1 = sb("s1", [P, 4, T])
        s2 = sb("s2", [P, 4, T])
        s3 = sb("s3", [P, 4, T])
        root = sb("root", [P, T])
        rstd = sb("rstd", [P, T])
        mod = sb("mod", [P, M_ALL])
        mod_step = sb("mod_step", [P, 8])
        cols = sb("cols", [P, C_ALL])
        consts = sb("consts", [P, K_ALL])
        co_a = sb("co_a", [P, NT])
        co_b = sb("co_b", [P, NT])
        co_a2 = sb("co_a2", [P, NT])
        co_b2 = sb("co_b2", [P, NT])
        co_g = sb("co_g", [P, NT])
        epsc = sb("epsc", [P, 2])
        scratch = sb("scratch", [P, 1])
        ones = sb("ones", [P, P])
        posi = sb("posi", [P, T], i32)
        table = sb("table", [P, T])
        krope = sb("krope", [ROPE, T])
        ubuf = sb("ubuf", [P, 4, 2, WIDTH - 1 + T])
        stat = sb("stat", [P, 3, 2, 2])
        ps = ctx.enter_context(nc.psum_tensor("ps", [P, 8, 512], f32))

        c_row = y[0:1, 0:D // T, :].rearrange("p t n -> p (t n)")
        yw = y[:, :, :].rearrange("p t n -> p (t n)")
        qn = yw[:, 0:512].rearrange("p (j n) -> p j n", j=2)
        qr = yw[0:ROPE, 512:1024].rearrange("p (j n) -> p j n", j=2)
        kn = yw[:, 1024:1536].rearrange("p (j n) -> p j n", j=2)
        vv = yw[:, 1536:2560].rearrange("p (b k n) -> p b k n", b=2, k=2)
        pr = yw[:, 2560:3328].rearrange("p (j n) -> p j n", j=2)
        prt = yw[:, 3328:4096].rearrange("p (j n) -> p j n", j=2)
        cq, ckv = hid[:, NT - RT:NT], xn[:, 0:RT]
        ident = consts[:, K_IDENT:K_IDENT + P]
        mask = consts[:, K_MASK:K_MASK + 3 * P].rearrange("p (o n) -> p o n", o=1)

        small_loaded, c_loaded = sem("small_loaded"), sem("c_loaded")
        h_loaded = [sem(f"h_loaded{q}") for q in range(4)]
        w_loaded = [sem(f"w_loaded{s}") for s in range(4)]
        ada_loaded = [sem(f"ada_loaded{s}") for s in range(2)]
        ada_used = sem("ada_used")
        mod_kept = sem("mod_kept")
        c_wide = sem("c_wide")
        c_ready = sem("c_ready")
        hi_ready = sem("hi_ready")
        lo_ready = sem("lo_ready")
        split_used = sem("split_used")
        low_copied = sem("low_copied")
        summed = sem("summed")
        evac_done = sem("evac_done")
        hid_hi = sem("hid_hi")
        hid_ready = sem("hid_ready")
        native_used = sem("native_used")
        diag_ready = sem("diag_ready")
        pe_taps = sem("pe_taps")
        conv_done = sem("conv_done")
        xin_ready = sem("xin_ready")
        sig_ready = sem("sig_ready")
        u_ready = sem("u_ready")
        taps = sem("taps")
        squares = sem("squares")
        partial = sem("partial")
        total = sem("total")
        root_ready = sem("root_ready")
        rstd_ready = sem("rstd_ready")
        y_scaled = sem("y_scaled")
        gates_ready = sem("gates_ready")
        start_normed = sem("start_normed")
        coef_ready = sem("coef_ready")
        centred = sem("centred")
        scaled = sem("scaled")
        silu_done = sem("silu_done")
        h_ready = sem("h_ready")
        xf_ready = sem("xf_ready")
        input_made = sem("input_made")
        xhi = sem("xhi")
        x_ready = sem("x_ready")
        step_done = sem("step_done")
        trig = sem("trig")
        ang = sem("ang")
        kv_copied = sem("kv_copied")
        q_copied = sem("q_copied")
        q_ready = sem("q_ready")
        q_step = sem("q_step")
        scores = sem("scores")
        masked = sem("masked")
        maxed = sem("maxed")
        exps = sem("exps")
        sums_inverted = sem("sums_inverted")
        probs_ready = sem("probs_ready")
        turned = sem("turned")
        prt_ready = sem("prt_ready")
        o_done = sem("o_done")
        o_hi = sem("o_hi")
        o_ready = sem("o_ready")
        y_cleared = sem("y_cleared")
        stored = sem("stored")

        def banks_of(g):
            return 4 * (g % 2)
        sum_bank = {S_H0: 6, S_MU: 6, S_VAR: 6, S_CQ: 5, S_CKV: 5}
        for y_sum, h_sum, g_next in ((S_Y0, S_H1, G_MLP0), (S_Y1, S_H2, G_DQ), (S_Y2, S_H3, G_MLP1), (S_Y3, None, G_MLP1 + 8 * CHUNKS)):
            sum_bank[y_sum], sum_bank[h_sum] = banks_of(g_next), banks_of(g_next - 1)
        LAST_OF = {G_MLP0: S_Y0, G_DQ: S_Y1, G_MLP1: S_Y2, G_MLP1 + 8 * CHUNKS: S_Y3}

        def before(counts, k):
            return sum(counts[:k])

        def inverses(k):
            return k + 1 if k < S_MU else k

        def in_bank(g):
            return 2 * g if g < START_GROUPS else 2 * (g % 2)

        def product_end(g):
            return GP * (START_GROUPS - 1) + g + 1 if g < START_GROUPS else GP * (g + 1)

        TAP_BANKS = (4, 5, 7, 4, 5, 7, 0, 2)
        SCORE_BANK, TURNED_BANK, K_BANK, V_BANK, Q_BANK, QR_BANK = 0, 2, 4, 5, 6, 7

        def out_bank(more):
            return Q_BANK if more else SCORE_BANK

        LOAD_LEAD = 4
        SPREADS = {0: (), 1: (0, 1), 2: (1, 1), 3: (1, 1, 1), 4: (2, 2)}

        def group_order(pieces, adas, lead=2):
            after = SPREADS[adas]
            out, a = [], 0
            for k in range(pieces):
                out.append(("w", k + lead))
                fill = adas if k == pieces - 1 else sum(after[:k + 1])
                out += [("a", x) for x in range(a, fill)]
                a = fill
            return out

        def not_yet(order, kind):
            if kind == "wo":
                adas, pieces = [x for x in order if x[0] == "a"], [("w", 4), ("w", 5)]
                return adas[:1] + pieces[:1] + adas[1:2] + pieces[1:] + adas[2:]
            return order[1:] if kind == "out" else order

        def run_order(order, p, a, do_w, do_a):
            for kind, k in order:
                if kind == "w":
                    if p.loops or p.static + k < N_ALL:
                        do_w(ahead(p, k))
                else:
                    do_a(ahead(a, k))

        def looped(eng, count, body):
            body(None)
            with eng.Fori(1, count) as i:
                body(i)

        def mlp(eng, group, g0, n0, a0, ups, downs, last_ups, u0):
            per = 4 * (ups + downs)

            def two(kind, c, i, u):
                off, a_off, adas = (0, 0, ups) if kind == "up" else (4, 4 * ups, downs)
                for j in range(2):
                    k = off + j
                    group(kind, at_loop(g0 + k, (8, c), (2, i)), at_loop(n0 + GP * k, (8 * GP, c), (2 * GP, i)),
                          at_loop(a0 + a_off + adas * j, (per, c), (2 * adas, i)), adas, at_loop(j, (2, i)), u, None)

            with eng.Fori(0, CHUNKS - 1) as c:
                with eng.Fori(0, 2) as i:
                    two("up", c, i, at_loop(u0, (4, c)))
                with eng.Fori(0, 2) as i:
                    two("down", c, i, at_loop(u0, (4, c)))
            k, ups = CHUNKS - 1, last_ups
            g0, n0, a0, u = g0 + 8 * k, n0 + 8 * GP * k, a0 + per * k, fixed(u0 + 4 * k)
            with eng.Fori(0, 2) as i:
                two("up", None, i, u)
            for k in range(4):
                group("down", fixed(g0 + 4 + k), fixed(n0 + GP * (4 + k)), fixed(a0 + 4 * ups + downs * k), downs, fixed(k), u, k)

        block = ctx.enter_context(nc.Block())

        @block.sync
        def _(sp):
            def load_w(p):
                s, n = p.static % 4, p.static
                if not p.loops and n < 4:
                    sp.wait_ge(ada_used, n + 3)
                elif n - 4 < N_OUT:
                    sp.wait_ge(native_used, value(p, -3))
                else:
                    sp.wait_ge(lo_ready, value(p, -3 - N_OUT, 2))
                sp.dma_start(raw[:, s, :], w_stream[value(p)]).then_inc(w_loaded[s], 16)

            def load_a(a):
                s = a.static % 2
                sp.wait_ge(ada_used, value(a, -1))
                sp.dma_start(ada[:, s, :], ada_stream[value(a)]).then_inc(ada_loaded[s], 16)

            def load_start(a):
                if 2 <= a < 6:
                    sp.dma_start(raw[:, a - 2, :], ada_stream[a]).then_inc(w_loaded[a - 2], 16)
                else:
                    if a >= 6:
                        sp.wait_ge(ada_used, a - 5 if a < 8 else a - 1)
                    sp.dma_start(ada[:, a % 2, :], ada_stream[a]).then_inc(ada_loaded[a % 2], 16)

            sp.dma_start(c_row, c.rearrange("(o n) -> o n", o=1)).then_inc(c_loaded, 16)
            sp.dma_start(cols[:, :], cols_d).then_inc(small_loaded, 16)
            sp.dma_start(consts[:, :], consts_d).then_inc(small_loaded, 16)
            sp.dma_start(posi[:, :], pos.rearrange("(o n) -> o n", o=1).broadcast_to([P, T])).then_inc(small_loaded, 16)
            for q in range(4):
                sp.dma_start(h[:, 4 * q:4 * q + 4, :], x_t[:, 4 * q:4 * q + 4, :]).then_inc(h_loaded[q], 16)
            for q in range(5):
                for k in range(8):
                    if q and k % 2 == 0:
                        load_w(fixed(4 * (q - 1) + k // 2))
                    if q < 4:
                        load_start(8 * q + k)

            def group(kind, g, n, a, per, t, u, q):
                run_order(group_order(GP, per, LOAD_LEAD), n, a, load_w, load_a)

            n, a = N_IN + GP * START_GROUPS, A_IN
            for kind in "waawaaww" + "waawaaww" + "aaaa" + "wawaww" + "aaaa" + "wwaaww" + 12 * "a":
                if kind == "w":
                    load_w(fixed(n))
                    n += 1
                else:
                    load_a(fixed(a))
                    a += 1
            for k in range(LOAD_LEAD):
                load_w(fixed(N_OUT + k))
            for k in range(A_OUT - A_LN):
                load_a(fixed(A_LN + k))
            for k in range(4):
                group("out", None, fixed(N_OUT + GP * k), fixed(A_OUT + A_OUT_GROUP * k), A_OUT_GROUP, fixed(k), None, k)
            mlp(sp, group, G_MLP0, N_MLP0, A_M0, A_UP, A_DOWN, A_UP + 1, 0)
            run_order(group_order(GP, 0, LOAD_LEAD), fixed(N_DQ), None, load_w, load_a)
            run_order(group_order(1, 0, LOAD_LEAD), fixed(N_KR), None, load_w, load_a)
            run_order(group_order(GP, 4, LOAD_LEAD), fixed(N_DKV), fixed(A_DKV), load_w, load_a)

            def pairs(i, off):
                for k in range(2):
                    run_order(group_order(2, A_PER_PAIR, LOAD_LEAD), at_loop(N_PAIR + 4 * off + 2 * k, (4, i)),
                              at_loop(A_PAIR + A_PER_PAIR * (2 * off + k), (2 * A_PER_PAIR, i)), load_w, load_a)
            looped(sp, 3, lambda i: pairs(i, 0))
            pairs(None, 3)

            for k in range(4):
                group("wo", None, fixed(N_WO + GP * k), fixed(A_WO + A_WO_GROUP * k), A_WO_GROUP, fixed(k), None, k)
            mlp(sp, group, G_MLP1, N_MLP1, A_M1, 1, 0, 1, 16)
            for q in range(4):
                sp.wait_ge(h_ready, 12 + q + 1)
                sp.dma_start(out_t[:, 4 * q:4 * q + 4, :], h[:, 4 * q:4 * q + 4, :]).then_inc(stored, 16)
            sp.wait_ge(stored, 64)

        @block.scalar
        def _(act):
            def split_hi(p):
                s, d = p.static % 4, p.static % 2
                act.wait_ge(w_loaded[s], value(turn(p, 4), 2, 16))
                for half in range(2):
                    at = slice(half * PIECE // 2, (half + 1) * PIECE // 2)
                    wait(act, split_used, value(p, -N_OUT, 2) - 3 + half)
                    act.activation(wsp[:, d, 0, at], raw[:, s, at], ACT.Copy).then_inc(hi_ready, 1)

            def halves(g, n, b, tiles=4, pieces=GP):
                act.wait_ge(split_used, value(n, pieces - N_OUT, 2))
                wait(act, summed, value(g))
                act.activation(s1[:, 0:tiles, :], ps[:, b:b + tiles, T:2 * T], ACT.Copy).then_inc(low_copied, 1)

            def quarter(buf, q):
                return buf[:, 4 * q:4 * q + 4, :]

            def square_y(k, q, g):
                act.wait_ge(evac_done, g + 1)
                wait(act, partial, before(PARTIALS, k) + q)
                act.activation(s3[:, :, :], quarter(y, q), ACT.Square).then_inc(squares, 1)
                act.wait_ge(squares, before(SQUARES, k) + q + 1)
                act.wait_ge(gates_ready, {S_Y0: 1, S_Y1: 2, S_Y2: 3, S_Y3: 4}[k])
                for t in range(4 * q, 4 * q + 4):
                    last = act.activation(y[:, t, :], y[:, t, :], ACT.Copy, scale=co_g[:, t:t + 1])
                last.then_inc(y_scaled, 1)

            def group(kind, g, n, a, per, t, u, q):
                order = group_order(GP, 0)
                if q == 0:
                    order = not_yet(order, kind)
                late = order[-1:] if q == 3 else []
                run_order(order[:len(order) - len(late)], n, a, split_hi, None)
                halves(g, n, 4 * (g.static % 2))
                run_order(late, n, a, split_hi, None)
                if kind == "up":
                    act.wait_ge(evac_done, value(g, 1))
                    act.activation(hid[:, bass.ds(value(t, 0, 4), 4), 0, :], s2[:, :, :], ACT.Copy).then_inc(hid_hi, 1)
                elif q is not None:
                    square_y(LAST_OF[g.static - q + 4], q, g.static)

            def square(k, q, src, ready, at):
                act.wait_ge(ready, at)
                wait(act, total, before(BATCHES, k))
                act.activation((s3, s0, s1, s2)[q][:, :, :], src, ACT.Square).then_inc(squares, 1)

            def load_root_table():
                act.activation(scratch[:, :], epsc[:, 0:1], ACT.Sqrt)

            def take_root(k, n):
                act.wait_ge(total, before(BATCHES, k + 1))
                wait(act, rstd_ready, inverses(k - 1) if k else 0)
                act.activation(root[:, :], ps[:, sum_bank[k], 0:T], ACT.Sqrt, bias=epsc[:, 0:1], scale=1.0 / n).then_inc(root_ready, 1)

            def shifted(dst, cb_, i):
                for q in range(4):
                    act.wait_ge(xf_ready, i + q + 1)
                    for t in range(4 * q, 4 * q + 4):
                        last = act.activation(dst[:, t, 0, :], y[:, t, :], ACT.Identity, bias=cb_[:, t:t + 1])
                    last.then_inc(xhi, 1)

            act.wait_ge(c_wide, 1)
            act.activation(cb[:, :], ps[:, 0:4, :].rearrange("p b n -> p (b n)"), ACT.Silu).then_inc(c_ready, 1)
            act.wait_ge(ang, 1)
            act.activation(table[64:128, :], rstd[64:128, :], ACT.Sin, scale=consts[64:128, K_SIGN:K_SIGN + 1]).then_inc(trig, 1)
            act.wait_ge(ang, 2)
            act.activation(table[0:64, :], root[0:64, :], ACT.Sin, scale=-1.0, bias=epsc[0:64, 1:2]).then_inc(trig, 1)
            for q in range(4):
                square(S_H0, q, quarter(h, q), h_loaded[q], 16)
            take_root(S_H0, D)

            def diagonals(g):
                wait(act, pe_taps, g - 1)
                for t in range(2):
                    for w in range(PE_TAPS):
                        c0 = C_CONV + CONV * g + GT + t * (WIDTH + 1) + w
                        made = act.activation(diag[g % 2][:, t, w, :], ident, ACT.Copy, scale=cols[:, c0:c0 + 1])
                made.then_inc(diag_ready, 1)

            def gate_half(g):
                wait(act, native_used, product_end(g))
                wait(act, u_ready, g - 1)
                for t in range(2):
                    c0 = C_CONV + CONV * g + 2 + t
                    last = act.activation(s1[:, 2 * (g % 2) + t, :], ps[:, in_bank(g) + 1, T * t:T * t + T], ACT.Sigmoid,
                                          bias=cols[:, c0:c0 + 1])
                last.then_inc(sig_ready, 1)

            for q in range(4):
                act.wait_ge(start_normed, q + 1)
                act.wait_ge(coef_ready, q + 1)
                for t in range(4 * q, 4 * q + 4):
                    last = act.activation(xf[:, t, :], y[:, t, :], ACT.Identity, scale=co_a[:, t:t + 1], bias=co_b[:, t:t + 1])
                last.then_inc(xin_ready, 1)
            for kind, g in ("g0", "g1", "g2", "d0", "g3", "d1", "g4", "d2", "g5", "d3", "g6", "d4", "g7", "d5", "d6", "d7"):
                (gate_half if kind == "g" else diagonals)(int(g))
            split_hi(fixed(N_OUT))
            split_hi(fixed(N_OUT + 1))

            act.wait_ge(total, before(BATCHES, S_MU + 1))
            act.wait_ge(rstd_ready, inverses(S_H0))
            load_root_table()
            act.activation(root[:, :], ps[:, sum_bank[S_MU], 0:T], ACT.Copy, scale=1.0 / D).then_inc(root_ready, 1)
            for q in range(4):
                square(S_VAR, q, quarter(y, q), centred, q + 1)
            take_root(S_VAR, D)
            for q in range(4):
                if q == 3:
                    split_hi(fixed(N_OUT + 2))
                act.wait_ge(scaled, q + 1)
                for t in range(4 * q, 4 * q + 4):
                    last = act.activation(y[:, t, :], y[:, t, :], ACT.Silu, bias=cols[:, C_LNB + t:C_LNB + t + 1],
                                          scale=cols[:, C_LNG + t:C_LNG + t + 1])
                last.then_inc(silu_done, 1)
                act.wait_ge(silu_done, q + 1)
                act.activation(hid[:, 4 * q:4 * q + 4, 0, :], quarter(y, q), ACT.Copy).then_inc(xhi, 1)

            load_root_table()
            for k in range(4):
                group("out", fixed(G_OUT + k), fixed(N_OUT + GP * k), None, 0, None, None, k)

            def post_and_pre(ky, kh, r, outs):
                take_root(ky, D)
                if kh is None:
                    return
                for q in range(4):
                    square(kh, q, quarter(h, q), h_ready, 4 * r + q + 1)
                take_root(kh, D)
                for dst, cb_, i in outs:
                    shifted(dst, cb_, i)

            post_and_pre(S_Y0, S_H1, 0, [(xn, co_b, 0)])
            mlp(act, group, G_MLP0, N_MLP0, A_M0, A_UP, A_DOWN, A_UP + 1, 0)
            post_and_pre(S_Y1, S_H2, 1, [])

            def input_high(dst, q, i):
                act.wait_ge(input_made, i - 8 + q + 1)
                act.activation(dst[:, 4 * q:4 * q + 4, 0, :], (s1, s2)[q % 2][:, :, :], ACT.Copy).then_inc(xhi, 1)
            for q in range(4):
                input_high(hid, q, 8)
            split_hi(fixed(N_DQ + 2))
            input_high(xn, 0, 12)
            input_high(xn, 1, 12)
            split_hi(fixed(N_DQ + 3))
            input_high(xn, 2, 12)
            input_high(xn, 3, 12)
            split_hi(fixed(N_DQ + 4))
            split_hi(fixed(N_DQ + 5))
            act.wait_ge(x_ready, 16)
            halves(fixed(G_DQ), fixed(N_DQ), banks_of(G_DQ))

            def rank_square(k, i, at):
                act.wait_ge(summed, at)
                wait(act, total, before(BATCHES, k))
                act.activation(s3[:, :, :], s0[:, :, :], ACT.Square).then_inc(squares, 1)

            def rank_high(i, dst):
                act.wait_ge(xf_ready, 8 + i + 1)
                act.activation(dst[:, :, 0, :], quarter(y, 2 * i), ACT.Copy).then_inc(xhi, 1)

            split_hi(fixed(N_KR + 2))
            rank_square(S_CQ, 0, G_DQ + 1)
            halves(fixed(G_KR), fixed(N_KR), banks_of(G_KR), 1, 1)
            split_hi(fixed(N_DKV + 2))
            take_root(S_CQ, RANK)
            rank_high(0, cq)
            split_hi(fixed(N_DKV + 3))
            split_hi(fixed(N_DKV + 4))
            halves(fixed(G_DKV), fixed(N_DKV), banks_of(G_DKV))
            split_hi(fixed(N_DKV + 5))
            rank_square(S_CKV, 1, G_DKV + 1)
            take_root(S_CKV, RANK)
            rank_high(1, ckv)

            def evac_q(p):
                act.wait_ge(split_used, value(p, 0, 4) + 2 * (N_PAIR - N_OUT + 1))
                act.wait_ge(x_ready, 18)
                wait(act, scores, value(p))
                act.activation(qn, ps[:, Q_BANK, :].rearrange("p (j n) -> p j n", j=2), ACT.Copy).then_inc(q_copied, 1)

            def evac_kv(p):
                b = p.static % 2
                act.wait_ge(split_used, value(p, 1, 4) + 2 * (N_PAIR - N_OUT))
                wait(act, scores, value(p))
                act.activation(kn, ps[:, K_BANK, :].rearrange("p (j n) -> p j n", j=2), ACT.Copy)
                wait(act, o_done, value(p, -1))
                act.activation(vv[:, b], ps[:, V_BANK, :].rearrange("p (j n) -> p j n", j=2), ACT.Copy).then_inc(kv_copied, 1)

            def pair(p, n, more):
                split_hi(ahead(n, 3))
                act.wait_ge(maxed, value(p, 1, 2))
                for j in range(2):
                    for t in range(2):
                        lo, hi = (0, P) if t == 0 else (P, 3 * P)
                        last = act.activation(pr[:, j, lo:hi], pr[:, j, lo:hi], ACT.Exp, bias=stat[:, 0, j, t:t + 1],
                                              scale=SCALE, accum_out=stat[:, 1, j, t:t + 1])
                last.then_inc(exps, 1)
                act.wait_ge(sums_inverted, value(p, 1))
                for j in range(2):
                    for t in range(2):
                        lo, hi = (0, P) if t == 0 else (P, 3 * P)
                        last = act.activation(pr[:, j, lo:hi], pr[:, j, lo:hi], ACT.Copy, scale=stat[:, 2, j, t:t + 1])
                last.then_inc(probs_ready, 1)
                if more:
                    evac_q(ahead(p, 1))
                else:
                    split_hi(ahead(n, 4))
                act.wait_ge(turned, value(p, 1))
                wait(act, o_done, value(p))
                act.activation(prt, ps[:, TURNED_BANK:TURNED_BANK + 2, 0:3 * P], ACT.Copy).then_inc(prt_ready, 1)
                if more:
                    split_hi(ahead(n, 4))
                    evac_kv(ahead(p, 1))
                act.wait_ge(o_done, value(p, 1))
                act.activation(hid[:, bass.ds(value(p, 0, 2), 2), 0, :], ps[:, out_bank(more), :].rearrange("p (j n) -> p j n", j=2), ACT.Copy).then_inc(o_hi, 1)
                if not more:
                    split_hi(ahead(n, 5))

            evac_q(fixed(0))
            split_hi(fixed(N_PAIR + 2))
            evac_kv(fixed(0))
            looped(act, 3, lambda i: [pair(at_loop(k, (2, i)), at_loop(N_PAIR + 2 * k, (4, i)), True) for k in range(2)])
            pair(fixed(6), fixed(N_PAIR + 12), True)
            pair(fixed(7), fixed(N_PAIR + 14), False)

            load_root_table()
            for k in range(4):
                group("wo", fixed(G_WO + k), fixed(N_WO + GP * k), None, 0, None, None, k)
            post_and_pre(S_Y2, S_H3, 2, [(xn, co_b, 10)])
            mlp(act, group, G_MLP1, N_MLP1, A_M1, 1, 0, 1, 16)
            post_and_pre(S_Y3, None, 3, [])

        @block.vector
        def _(ve):
            steps = [0]

            def step(ins):
                steps[0] += 1
                ins.then_inc(step_done, 1)

            def settled():
                ve.wait_ge(step_done, steps[0])

            def split_lo(p):
                s, d = p.static % 4, p.static % 2
                for half in range(2):
                    at = slice(half * PIECE // 2, (half + 1) * PIECE // 2)
                    ve.wait_ge(hi_ready, value(p, -N_OUT, 2) + half + 1)
                    ve.tensor_tensor(wsp[:, d, 1, at], raw[:, s, at], wsp[:, d, 0, at].bitcast(f32), ALU.subtract).then_inc(lo_ready, 1)

            def mod_column(a):
                if not a.loops:
                    return mod[:, a.static:a.static + 1]
                return mod_step[:, a.static % 8:a.static % 8 + 1]

            def keep_mod(a, per):
                if a.loops and per:
                    ve.wait_ge(ada_used, value(a, per))
                    for k in range(per):
                        c0 = (a.static + k) % 8
                        last = ve.tensor_copy(mod[:, bass.ds(value(a, k), 1)], mod_step[:, c0:c0 + 1])
                    last.then_inc(mod_kept, 1)

            def reduce_ada(a):
                s = a.static % 2
                ve.wait_ge(ada_loaded[s], value(turn(ahead(a, -4), 2), 1, 16))
                ve.tensor_tensor_reduce(out=ada[:, s, :], in0=ada[:, s, :], in1=cb[:, :], scale=1.0, scalar=0.0,
                                        op0=ALU.mult, op1=ALU.add, accum_out=mod_column(a)).then_inc(ada_used, 1)

            def add_halves(g, b):
                ve.wait_ge(low_copied, value(g, 1))
                wait(ve, evac_done, value(g))
                ve.tensor_tensor(s0[:, :, :], ps[:, b:b + 4, 0:T], s1[:, :, :], ALU.add).then_inc(summed, 1)
                ve.wait_ge(summed, value(g, 1))

            def sum_quarter(k, q):
                ve.wait_ge(squares, before(SQUARES, k) + q + 1)
                ve.tensor_reduce(s2[:, q, :], s3[:, :, :].rearrange("p t n -> p n t"), AX.X, ALU.add).then_inc(partial, 1)

            def group(kind, g, n, a, per, t, u, q):
                order = group_order(GP, per)
                if q == 0:
                    order = not_yet(order, kind)
                if q == 0:
                    gate_gain(LAST_OF[g.static + 4])
                if q:
                    run_order(order[:2], n, a, split_lo, reduce_ada)
                    sum_quarter(LAST_OF[g.static - q + 4], q - 1)
                    order = order[2:]
                late = order[-1:] if q == 3 else []
                run_order(order[:len(order) - len(late)], n, a, split_lo, reduce_ada)
                keep_mod(a, per)
                add_halves(g, 4 * (g.static % 2))
                at = bass.ds(value(t, 0, 4), 4)
                if kind == "out":
                    bias = cols[:, C_BOUT + 4 * q:C_BOUT + 4 * q + 4].rearrange("p (t o) -> p t o", o=1).broadcast_to([P, 4, T])
                    ve.tensor_tensor(quarter(y, q), s0[:, :, :], bias, ALU.add).then_inc(evac_done, 1)
                elif kind == "wo":
                    ve.tensor_copy(quarter(y, q), s0[:, :, :]).then_inc(evac_done, 1)
                elif kind == "down":
                    ve.wait_ge(y_cleared, 1 if g.static < G_DQ else 2)
                    ve.tensor_tensor(y[:, at, :], y[:, at, :], s0[:, :, :], ALU.add).then_inc(evac_done, 1)
                if kind != "up":
                    run_order(late, n, a, split_lo, reduce_ada)
                    return
                done = value(u) + value(t)
                ve.scalar_tensor_tensor(s2[:, :, :], s0[:, :, :], 0.0, s0[:, :, :], ALU.max, ALU.mult).then_inc(evac_done, 1)
                ve.wait_ge(hid_hi, done + 1)
                ve.tensor_tensor(hid[:, at, 1, :], s2[:, :, :], hid[:, at, 0, :].bitcast(f32), ALU.subtract).then_inc(hid_ready, 1)
                ve.wait_ge(hid_ready, done + 1)

            def quarter(buf, q):
                return buf[:, 4 * q:4 * q + 4, :]

            def invert(k):
                ve.wait_ge(root_ready, k + 1)
                ve.reciprocal(rstd[:, :], root[:, :]).then_inc(rstd_ready, 1)
                ve.wait_ge(rstd_ready, inverses(k))

            def wide(row, n=4):
                return row[:, :].rearrange("p (o n) -> p o n", o=1).broadcast_to([P, n, T])

            def scale_shift(ca, cb_, m, gain):
                step(ve.tensor_tensor(cb_[:, :], mod[:, m:m + NT], cols[:, C_BADA + m:C_BADA + m + NT], ALU.add))
                step(ve.tensor_tensor(ca[:, :], mod[:, m + NT:m + 2 * NT], cols[:, C_BADA + m + NT:C_BADA + m + 2 * NT], ALU.add))
                settled()
                step(ve.scalar_tensor_tensor(ca[:, :], ca[:, :], 1.0, cols[:, gain:gain + NT], ALU.add, ALU.mult))
                settled()

            def gate_gain(k):
                m, gain, used, kept = {
                    S_Y0: (M_MIX0 + 32, C_POSTMIX, A_OUT, 0), S_Y1: (M_MLP0 + 32, C_POSTMLP, A_M0 + 16, 28),
                    S_Y2: (M_MIX1 + 32, C_POSTMIX + NT, A_WO, 32), S_Y3: (M_MLP1 + 32, C_POSTMLP + NT, M_ALL, 48)}[k]
                ve.wait_ge(ada_used, used)
                wait(ve, mod_kept, kept)
                step(ve.tensor_tensor(co_g[:, :], mod[:, m:m + NT], cols[:, C_BADA + m:C_BADA + m + NT], ALU.add))
                settled()
                ve.tensor_tensor(co_g[:, :], co_g[:, :], cols[:, gain:gain + NT], ALU.mult).then_inc(gates_ready, 1)

            def times_gain(ca, r):
                wait(ve, h_ready, 4 * r)
                for t in range(NT):
                    last = ve.tensor_scalar(y[:, t, :], h[:, t, :], ca[:, t:t + 1], None, ALU.mult)
                step(last)

            def modulated(k, dst, cb_, i):
                settled()

                def times(q):
                    ve.tensor_tensor(quarter(y, q), quarter(y, q), wide(rstd), ALU.mult).then_inc(xf_ready, 1)
                times(0)
                for q in range(4):
                    if q < 3:
                        times(q + 1)
                    ve.wait_ge(xhi, i + q + 1)
                    for t in range(4 * q, 4 * q + 4):
                        last = ve.scalar_tensor_tensor(dst[:, t, 1, :], y[:, t, :], cb_[:, t:t + 1], dst[:, t, 0, :].bitcast(f32),
                                                       ALU.add, ALU.subtract)
                    last.then_inc(x_ready, 1)

            def residual(k, r):
                invert(k)

                def times(q):
                    ve.wait_ge(y_scaled, 4 * r + q + 1)
                    step(ve.tensor_tensor(quarter(y, q), quarter(y, q), wide(rstd), ALU.mult))
                times(0)
                for q in range(4):
                    at = steps[0]
                    if q < 3:
                        times(q + 1)
                    ve.wait_ge(step_done, at)
                    ve.tensor_tensor(quarter(h, q), quarter(h, q), quarter(y, q), ALU.add).then_inc(h_ready, 1)

            ve.memset(epsc[:, 0:1], EPS)
            ve.memset(epsc[:, 1:2], float(np.pi / 2))
            step(ve.memset(ones[:, :], 1.0))
            ve.memset(ubuf[:, :, :], 0.0)
            ve.wait_ge(small_loaded, 48)
            step(ve.tensor_copy(rstd[:, :], posi[:, :]))
            settled()
            step(ve.tensor_scalar(rstd[:, :], rstd[:, :], consts[:, K_INV:K_INV + 1], None, ALU.mult))
            settled()
            magic = 1.5 * 2.0 ** 23
            step(ve.tensor_scalar(root[:, :], rstd[:, :], float(1 / (2 * np.pi)), magic, ALU.mult, ALU.add))
            settled()
            step(ve.tensor_scalar(root[:, :], root[:, :], magic, None, ALU.subtract))
            settled()
            part1 = 6.28125
            part2 = float(np.float32(np.round((2 * np.pi - part1) * 2 ** 22) / 2 ** 22))
            part3 = float(2 * np.pi - part1 - part2)
            for part in (part1, part2, part3):
                step(ve.scalar_tensor_tensor(rstd[:, :], root[:, :], -part, rstd[:, :], ALU.mult, ALU.add))
                settled()
            below = float(np.nextafter(np.float32(np.pi), np.float32(0)))
            ve.tensor_scalar(rstd[:, :], rstd[:, :], below, -below, ALU.min, ALU.max).then_inc(ang, 1)
            ve.wait_ge(ang, 1)
            ve.scalar_tensor_tensor(root[:, :], rstd[:, :], -1.0, rstd[:, :], ALU.mult, ALU.max).then_inc(ang, 1)

            ve.wait_ge(c_ready, 1)
            for q in range(4):
                for a in range(8 * q, 8 * q + 8):
                    m = M_MIX0 + 4 * q + a % 4 + (NT if a % 8 >= 4 else 0)
                    if 2 <= a < 6:
                        buf = raw[:, a - 2, :]
                        ve.wait_ge(w_loaded[a - 2], 16)
                    else:
                        buf = ada[:, a % 2, :]
                        ve.wait_ge(ada_loaded[a % 2], 16 if a < 2 else 16 * ((a - 4) // 2 + 1))
                    ve.tensor_tensor_reduce(out=buf, in0=buf, in1=cb[:, :], scale=1.0, scalar=0.0,
                                            op0=ALU.mult, op1=ALU.add, accum_out=mod[:, m:m + 1]).then_inc(ada_used, 1)
                    if a == 2:
                        invert(S_H0)
                    if a in (2, 9, 11, 13):
                        k = max(a - 7, 0) // 2
                        ve.tensor_tensor(quarter(y, k), quarter(h, k), wide(rstd), ALU.mult).then_inc(start_normed, 1)
                ve.wait_ge(ada_used, 8 * q + 8)
                at = slice(4 * q, 4 * q + 4)
                shift, scale = slice(M_MIX0 + 4 * q, M_MIX0 + 4 * q + 4), slice(M_MIX0 + NT + 4 * q, M_MIX0 + NT + 4 * q + 4)
                step(ve.tensor_tensor(co_b[:, at], mod[:, shift], cols[:, shift], ALU.add))
                step(ve.tensor_tensor(co_a[:, at], mod[:, scale], cols[:, scale], ALU.add))
                settled()
                ve.scalar_tensor_tensor(co_a[:, at], co_a[:, at], 1.0, cols[:, C_PREMIX + 4 * q:C_PREMIX + 4 * q + 4],
                                        ALU.add, ALU.mult).then_inc(coef_ready, 1)

            def accumulator(g):
                return (s2, s0)[g // 2 % 2][:, 2 * (g % 2):2 * (g % 2) + 2, :]

            OWN = 2 * (WIDTH - PE_TAPS)

            def gated(g):
                ve.wait_ge(sig_ready, g + 1)
                wait(ve, taps, OWN * (g - 3))
                wait(ve, pe_taps, g - 3)
                for t in range(2):
                    c0 = C_CONV + CONV * g + t
                    last = ve.scalar_tensor_tensor(ubuf[:, g % 4, t, WIDTH - 1:], ps[:, in_bank(g), T * t:T * t + T], cols[:, c0:c0 + 1],
                                                   s1[:, 2 * (g % 2) + t, :], ALU.add, ALU.mult)
                last.then_inc(u_ready, 1)

            def finish_conv(g):
                ve.wait_ge(taps, OWN * (g + 1))
                ve.wait_ge(pe_taps, g + 1)
                ve.tensor_tensor(y[:, 2 * g:2 * g + 2, :], accumulator(g),
                                 ps[:, TAP_BANKS[g], :].rearrange("p (t n) -> p t n", t=2), ALU.add).then_inc(conv_done, 1)

            def add_taps(g):
                for k in range(A_CONV // 2):
                    reduce_ada(fixed(A_IN + A_CONV * g + k))
                if g >= 4:
                    finish_conv(g - 4)
                    ve.wait_ge(conv_done, g - 3)
                ve.wait_ge(u_ready, g + 1)
                for w in range(PE_TAPS, WIDTH):
                    if w == (PE_TAPS + WIDTH) // 2:
                        for k in range(A_CONV // 2, A_CONV):
                            reduce_ada(fixed(A_IN + A_CONV * g + k))
                    for t in range(2):
                        acc, u = accumulator(g)[:, t, :], ubuf[:, g % 4, t, w:w + T]
                        c0 = C_CONV + CONV * g + GT + t * (WIDTH + 1)
                        if w == PE_TAPS:
                            ve.tensor_scalar(acc, u, cols[:, c0 + w:c0 + w + 1], cols[:, c0 + WIDTH:c0 + WIDTH + 1],
                                             ALU.mult, ALU.add).then_inc(taps, 1)
                            continue
                        ve.wait_ge(taps, OWN * g + 2 * (w - PE_TAPS - 1) + t + 1)
                        ve.scalar_tensor_tensor(acc, u, cols[:, c0 + w:c0 + w + 1], acc, ALU.mult, ALU.add).then_inc(taps, 1)

            for kind, g in ("g0", "t0", "g1", "g2", "g3", "t1", "t2", "g4", "t3", "g5", "t4", "t5", "g6", "t6", "g7", "t7"):
                (gated if kind == "g" else add_taps)(int(g))
            for g in range(IN_GROUPS - 4, IN_GROUPS - 1):
                finish_conv(g)
            split_lo(fixed(N_OUT))
            reduce_ada(fixed(A_LN))
            finish_conv(IN_GROUPS - 1)
            split_lo(fixed(N_OUT + 1))
            ve.wait_ge(root_ready, S_MU + 1)
            for q in range(4):
                ve.tensor_tensor(quarter(y, q), quarter(y, q), wide(root), ALU.subtract).then_inc(centred, 1)
            reduce_ada(fixed(A_LN + 1))
            reduce_ada(fixed(A_LN + 2))
            invert(S_VAR)
            for q in range(4):
                ve.tensor_tensor(quarter(y, q), quarter(y, q), wide(rstd), ALU.mult).then_inc(scaled, 1)
            for q in range(4):
                if q == 1:
                    reduce_ada(fixed(A_LN + 3))
                if q == 3:
                    split_lo(fixed(N_OUT + 2))
                ve.wait_ge(xhi, q + 1)
                ve.tensor_tensor(hid[:, 4 * q:4 * q + 4, 1, :], quarter(y, q), hid[:, 4 * q:4 * q + 4, 0, :].bitcast(f32),
                                 ALU.subtract).then_inc(x_ready, 1)

            for k in range(4):
                group("out", fixed(G_OUT + k), fixed(N_OUT + GP * k), fixed(A_OUT + A_OUT_GROUP * k), A_OUT_GROUP, fixed(k), None, k)

            ve.wait_ge(evac_done, G_MLP0)
            ve.wait_ge(ada_used, A_M0)
            scale_shift(co_a, co_b, M_MLP0, C_PREMLP)
            residual(S_Y0, 0)
            times_gain(co_a, 1)
            invert(S_H1)
            modulated(S_H1, xn, co_b, 4)
            ve.wait_ge(x_ready, 8)
            mlp(ve, group, G_MLP0, N_MLP0, A_M0, A_UP, A_DOWN, A_UP + 1, 0)

            ve.wait_ge(evac_done, G_DQ)
            ve.wait_ge(ada_used, A_DKV)
            scale_shift(co_a2, co_b2, M_MIX1, C_PREMIX + NT)
            scale_shift(co_a, co_b, M_KV, C_GKV)
            residual(S_Y1, 1)
            wait(ve, h_ready, 8)
            invert(S_H2)

            def made_input(ca, cb_, q, i):
                buf = (s1, s2)[q % 2]
                if i + q > 9:
                    ve.wait_ge(x_ready, i + q - 1)
                for t in range(4):
                    k = 4 * q + t
                    last = ve.tensor_scalar(buf[:, t, :], y[:, k, :], ca[:, k:k + 1], cb_[:, k:k + 1], ALU.mult, ALU.add)
                last.then_inc(input_made, 1)

            def normed(q):
                ve.tensor_tensor(quarter(y, q), quarter(h, q), wide(rstd), ALU.mult).then_inc(xf_ready, 1)
                ve.wait_ge(xf_ready, 4 + q + 1)
                made_input(co_a2, co_b2, q, 8)

            def low_part(dst, q, i):
                ve.wait_ge(xhi, i + q + 1)
                ve.tensor_tensor(dst[:, 4 * q:4 * q + 4, 1, :], (s1, s2)[q % 2][:, :, :], dst[:, 4 * q:4 * q + 4, 0, :].bitcast(f32),
                                 ALU.subtract).then_inc(x_ready, 1)
            normed(0)
            normed(1)
            low_part(hid, 0, 8)
            normed(2)
            low_part(hid, 1, 8)
            normed(3)
            low_part(hid, 2, 8)
            low_part(hid, 3, 8)
            split_lo(fixed(N_DQ + 2))
            for q in (0, 2):
                made_input(co_a, co_b, q, 12)
                made_input(co_a, co_b, q + 1, 12)
                low_part(xn, q, 12)
                low_part(xn, q + 1, 12)
                if q == 0:
                    split_lo(fixed(N_DQ + 3))
            split_lo(fixed(N_DQ + 4))
            split_lo(fixed(N_DQ + 5))

            def rank_sum(g, i, gain):
                add_halves(fixed(g), banks_of(g))
                ve.wait_ge(x_ready, 16)
                for t in range(RT):
                    last = ve.tensor_scalar(y[:, 8 * i + t, :], s0[:, t, :], cols[:, gain + t:gain + t + 1], None, ALU.mult)
                last.then_inc(evac_done, 1)
                ve.wait_ge(evac_done, g + 1)

            def rank_norm(k, i, dst):
                invert(k)
                ve.tensor_tensor(quarter(y, 2 * i), quarter(y, 2 * i), wide(rstd), ALU.mult).then_inc(xf_ready, 1)
                ve.wait_ge(xhi, 16 + i + 1)
                ve.tensor_tensor(dst[:, :, 1, :], quarter(y, 2 * i), dst[:, :, 0, :].bitcast(f32), ALU.subtract).then_inc(x_ready, 1)

            rank_sum(G_DQ, 0, C_GCQ)
            split_lo(fixed(N_KR + 2))
            b = banks_of(G_KR)
            ve.wait_ge(low_copied, G_KR + 1)
            ve.wait_ge(evac_done, G_KR)
            ve.wait_ge(squares, before(SQUARES, S_CQ + 1))
            ve.tensor_tensor(s0[:, 0, :], ps[:, b, 0:T], s1[:, 0, :], ALU.add).then_inc(summed, 1)
            ve.wait_ge(summed, G_KR + 1)
            step(ve.tensor_tensor(s2[0:ROPE, 0, :], s0[0:ROPE, 0, :], table[0:ROPE, :], ALU.mult))
            step(ve.tensor_tensor(s2[0:ROPE, 1, :], s0[ROPE:P, 0, :], table[ROPE:P, :], ALU.mult))
            settled()
            ve.tensor_tensor(krope[:, :], s2[0:ROPE, 0, :], s2[0:ROPE, 1, :], ALU.add).then_inc(evac_done, 1)
            split_lo(fixed(N_DKV + 2))
            rank_norm(S_CQ, 0, cq)
            split_lo(fixed(N_DKV + 3))
            reduce_ada(fixed(A_DKV))
            split_lo(fixed(N_DKV + 4))
            reduce_ada(fixed(A_DKV + 1))
            rank_sum(G_DKV, 1, C_GCKV)
            split_lo(fixed(N_DKV + 5))
            reduce_ada(fixed(A_DKV + 2))
            rank_norm(S_CKV, 1, ckv)
            reduce_ada(fixed(A_DKV + 3))

            def rotate_q(p):
                ve.wait_ge(split_used, value(p, 0, 4) + 2 * (N_PAIR - N_OUT + 1))
                wait(ve, scores, value(p))
                tab = table[:, :].rearrange("p (o n) -> p o n", o=1).broadcast_to([P, 2, T])
                both = ps[:, QR_BANK, :].rearrange("p (j n) -> p j n", j=2)
                wait(ve, q_ready, value(p))
                ve.tensor_tensor(s2[0:ROPE, 0:2, :], both[0:ROPE], tab[0:ROPE], ALU.mult).then_inc(q_step, 1)
                ve.tensor_tensor(s2[0:ROPE, 2:4, :], both[ROPE:P], tab[ROPE:P], ALU.mult).then_inc(q_step, 1)
                ve.wait_ge(q_step, value(p, 1, 2))
                ve.tensor_tensor(qr, s2[0:ROPE, 0:2, :], s2[0:ROPE, 2:4, :], ALU.add).then_inc(q_ready, 1)

            def pair(p, n, a, more):
                ve.wait_ge(scores, value(p, 1))
                wait(ve, turned, value(p))
                ve.tensor_tensor(pr, ps[:, SCORE_BANK:SCORE_BANK + 2, 0:3 * P], mask.broadcast_to([P, 2, 3 * P]), ALU.add).then_inc(masked, 1)
                ve.wait_ge(masked, value(p, 1))
                ve.tensor_reduce(stat[:, 0, :, 0], pr[:, :, 0:P], AX.X, ALU.max)
                ve.tensor_reduce(stat[:, 0, :, 1], pr[:, :, P:3 * P], AX.X, ALU.max).then_inc(maxed, 1)
                ve.wait_ge(maxed, value(p, 0, 2) + 1)
                ve.tensor_scalar(stat[:, 0, :, :], stat[:, 0, :, :], -SCALE, None, ALU.mult).then_inc(maxed, 1)
                split_lo(ahead(n, 3))
                ve.wait_ge(exps, value(p, 1))
                ve.reciprocal(stat[:, 2, :, :], stat[:, 1, :, :]).then_inc(sums_inverted, 1)
                if more:
                    rotate_q(ahead(p, 1))
                reduce_ada(a)
                split_lo(ahead(n, 4))
                reduce_ada(ahead(a, 1))
                ve.wait_ge(o_hi, value(p, 1))
                at = bass.ds(value(p, 0, 2), 2)
                ve.tensor_tensor(hid[:, at, 1, :], ps[:, out_bank(more), :].rearrange("p (j n) -> p j n", j=2), hid[:, at, 0, :].bitcast(f32),
                                 ALU.subtract).then_inc(o_ready, 1)
                if not more:
                    split_lo(ahead(n, 5))
                for k in range(2, A_PER_PAIR):
                    reduce_ada(ahead(a, k))
                keep_mod(a, A_PER_PAIR)

            rotate_q(fixed(0))
            split_lo(fixed(N_PAIR + 2))
            looped(ve, 3, lambda i: [pair(at_loop(k, (2, i)), at_loop(N_PAIR + 2 * k, (4, i)), at_loop(A_PAIR + A_PER_PAIR * k, (2 * A_PER_PAIR, i)), True)
                                     for k in range(2)])
            pair(fixed(6), fixed(N_PAIR + 12), fixed(A_PAIR + 6 * A_PER_PAIR), True)
            pair(fixed(7), fixed(N_PAIR + 14), fixed(A_PAIR + 7 * A_PER_PAIR), False)

            for k in range(4):
                group("wo", fixed(G_WO + k), fixed(N_WO + GP * k), fixed(A_WO + A_WO_GROUP * k), A_WO_GROUP, fixed(k), None, k)

            ve.wait_ge(evac_done, G_MLP1)
            ve.wait_ge(ada_used, A_M1)
            ve.wait_ge(mod_kept, 32)
            scale_shift(co_a, co_b, M_MLP1, C_PREMLP + NT)
            residual(S_Y2, 2)
            times_gain(co_a, 3)
            invert(S_H3)
            modulated(S_H3, xn, co_b, 18)
            ve.wait_ge(x_ready, 22)
            mlp(ve, group, G_MLP1, N_MLP1, A_M1, 1, 0, 1, 16)
            ve.wait_ge(evac_done, G_MLP1 + 8 * CHUNKS)
            residual(S_Y3, 3)

        @block.gpsimd
        def _(pool):
            for at in (8, 22):
                pool.wait_ge(x_ready, at)
                pool.memset(y[:, :, :], 0.0).then_inc(y_cleared, 1)

        @block.tensor
        def _(pe):
            def product(g, n, src, ready, at, between=None):
                b = 4 * (g.static % 2)
                wait(pe, summed, value(g, -1))

                def low(d, kt, o):
                    at_w = slice((kt % 4 * GT + o) * P, (kt % 4 * GT + o + 1) * P)
                    pe.matmul(ps[:, b + o, 0:T], wsp[:, d, 1, at_w], src[:, kt, 0, :], start=kt == 0, stop=False, skip_group_check=True)

                def high(d, kt, o):
                    at_w = slice((kt % 4 * GT + o) * P, (kt % 4 * GT + o + 1) * P)
                    return pe.matmul(ps[:, b + o, :], wsp[:, d, 0, at_w], src[:, kt, :, :].rearrange("p a n -> p (a n)"), start=False,
                                     stop=kt == NT - 1, skip_group_check=True)

                for j in range(GP):
                    if between and j in between:
                        between[j]()
                    d = (n.static + j) % 2
                    if j == 0:
                        if ready is x_ready:
                            pe.wait_ge(xhi, at + 1)
                        elif ready is not None:
                            pe.wait_ge(ready, at + 1)
                        for kt in range(4):
                            if kt % 2 == 0:
                                pe.wait_ge(lo_ready, value(n, -N_OUT, 2) + kt // 2 + 1)
                            for o in range(GT):
                                low(d, kt, o)
                    if ready is not None:
                        pe.wait_ge(ready, at + j + 1)
                    for k in range(4):
                        if j and k % 2 == 0:
                            pe.wait_ge(lo_ready, value(n, j - N_OUT, 2) + k // 2 + 1)
                        for o in range(GT):
                            if j:
                                low(d, 4 * j + k, o)
                            last = high(d, 4 * j + k, o)
                        if k % 2:
                            last.then_inc(split_used, 1)

            def over_partitions(k, src, first, end):
                return pe.matmul(ps[:, sum_bank[k], 0:T], ones[:, :], src, start=first, stop=end)

            def keep_warm(bank, n):
                for _ in range(n):
                    pe.matmul(ps[:, bank, :], ones[:, :], consts[:, K_IDENT:K_IDENT + 4 * P], start=True, stop=True)

            def sum_partials(k, g):
                pe.wait_ge(summed, g)
                pe.wait_ge(partial, before(PARTIALS, k + 1))
                for q in range(3):
                    over_partitions(k, s2[:, q, :], q == 0, False)

            def sum_y(k):
                keep_warm(sum_bank[k] + 1, 5)
                pe.wait_ge(squares, before(SQUARES, k + 1))
                for t in range(4):
                    last = over_partitions(k, s3[:, t, :], False, t == 3)
                last.then_inc(total, 1)

            def sum_quarters(k, warm=None):
                if warm:
                    keep_warm(warm, 3 if k == S_VAR else 5)
                for q in range(SQUARES[k]):
                    pe.wait_ge(squares, before(SQUARES, k) + q + 1)
                    for t in range(4):
                        last = over_partitions(k, (s3, s0, s1, s2)[q][:, t, :], q + t == 0, q == SQUARES[k] - 1 and t == 3)
                    last.then_inc(total, 1)
                if warm:
                    keep_warm(warm, 6)

            def with_partials(g, q):
                return {3: lambda: sum_partials(LAST_OF[g.static + 1], g.static)} if q == 3 else None

            def group(kind, g, n, a, per, t, u, q):
                if kind == "up":
                    product(g, n, xn, x_ready, 4 if g.static < G_DQ else 18)
                else:
                    product(g, n, hid, hid_ready, value(u), with_partials(g, q))

            pe.wait_ge(step_done, 1)
            pe.wait_ge(c_loaded, 16)
            for b in range(4):
                last = pe.matmul(ps[:, b, :], ones[0:1, :], c_row[:, 512 * b:512 * b + 512], start=True, stop=True)
            last.then_inc(c_wide, 1)
            pe.wait_ge(small_loaded, 48)
            sum_quarters(S_H0)

            def unsplit(g, n, j):
                s = n % 4
                pe.wait_ge(w_loaded[s], 16 * (n // 4 + 2))
                for k in range(4):
                    for o in range(GT):
                        kt, at_w = 4 * j + k, slice((k * GT + o) * P, (k * GT + o + 1) * P)
                        last = pe.matmul(ps[:, in_bank(g) + o // 2, T * (o % 2):T * (o % 2) + T], raw[:, s, at_w], xf[:, kt, :],
                                         start=kt == 0 and o % 2 == 0, stop=kt == NT - 1 and o % 2 == 1, skip_group_check=True)
                last.then_inc(native_used, 1)

            for j in range(GP):
                pe.wait_ge(xin_ready, j + 1)
                for g in range(START_GROUPS):
                    if g == 3 and j == 0:
                        pe.wait_ge(root_ready, 1)
                    unsplit(g, 4 * j + g, j)

            def in_product(g):
                pe.wait_ge(u_ready, {4: 1, 5: 2, 6: 5, 7: 6}[g])
                for j in range(GP):
                    unsplit(g, GP * g + j, j)

            def add_mean(g):
                pe.wait_ge(conv_done, g + 1)
                for t in range(2):
                    last = over_partitions(S_MU, y[:, 2 * g + t, :], g + t == 0, g == IN_GROUPS - 1 and t == 1)
                if g == IN_GROUPS - 1:
                    last.then_inc(total, 1)

            def add_taps(g):
                pe.wait_ge(diag_ready, g + 1)
                pe.wait_ge(u_ready, max(g + 1, START_GROUPS))
                if g < 6:
                    wait(pe, conv_done, g - 2)
                for t in range(2):
                    for w in range(PE_TAPS):
                        last = pe.matmul(ps[:, TAP_BANKS[g], T * t:T * t + T], diag[g % 2][:, t, w, :], ubuf[:, g % 4, t, w:w + T],
                                         start=w == 0, stop=w == PE_TAPS - 1)
                last.then_inc(pe_taps, 1)

            for kind, g in ("p4", "t0", "p5", "t1", "p6", "t2", "p7", "t3", "t4", "t5", "m0", "t6", "m1", "m2", "m3", "t7", "m4", "m5", "m6", "m7"):
                {"p": in_product, "t": add_taps, "m": add_mean}[kind](int(g))
            sum_quarters(S_VAR, 5)

            for k in range(4):
                product(fixed(G_OUT + k), fixed(N_OUT + GP * k), hid, x_ready, 0, with_partials(fixed(G_OUT + k), k))
            sum_y(S_Y0)
            sum_quarters(S_H1, sum_bank[S_Y0] + 1)
            mlp(pe, group, G_MLP0, N_MLP0, A_M0, A_UP, A_DOWN, A_UP + 1, 0)
            sum_y(S_Y1)
            sum_quarters(S_H2, sum_bank[S_Y1] + 1)

            product(fixed(G_DQ), fixed(N_DQ), hid, x_ready, 8)
            b, d = banks_of(G_KR), N_KR % 2
            for kt in range(NT):
                if kt % 4 == 0:
                    pe.wait_ge(x_ready, 12 + kt // 4 + 1)
                if kt % 8 == 0:
                    pe.wait_ge(lo_ready, 2 * (N_KR - N_OUT) + kt // 8 + 1)
                at_w = slice(kt * P, (kt + 1) * P)
                if kt:
                    pe.matmul(ps[:, b, 0:T], wsp[:, d, 1, at_w], xn[:, kt, 0, :], start=False, stop=False)
                last = pe.matmul(ps[:, b, :], wsp[:, d, 0, at_w], xn[:, kt, :, :].rearrange("p a n -> p (a n)"), start=kt == 0, stop=kt == NT - 1)
                if not kt:
                    last = pe.matmul(ps[:, b, 0:T], wsp[:, d, 1, at_w], xn[:, kt, 0, :], start=False, stop=False)
                if kt % 8 == 7:
                    last.then_inc(split_used, 1)

            def sum_rank(k):
                pe.wait_ge(squares, before(SQUARES, k + 1))
                for t in range(RT):
                    last = over_partitions(k, s3[:, t, :], t == 0, t == RT - 1)
                last.then_inc(total, 1)

            product(fixed(G_DKV), fixed(N_DKV), xn, None, 0, {1: lambda: sum_rank(S_CQ)})

            def three(bank, at, d, w_at, src):
                last = None
                for kt in range(RT):
                    wa = slice(kt * 512 + w_at, kt * 512 + w_at + P)
                    for m, (wi, xi) in enumerate(((0, 0), (0, 1), (1, 0))):
                        before_last, last = last, pe.matmul(ps[:, bank, at:at + T], wsp[:, d, wi, wa], src[:, kt, xi, :],
                                                            start=kt == 0 and m == 0, stop=kt == RT - 1 and m == 2)
                return before_last, last

            def project_q(p, n):
                wait(pe, q_copied, value(p))
                wait(pe, q_ready, value(p))
                wait(pe, o_ready, value(p, -1))
                d = n.static % 2
                pe.wait_ge(lo_ready, value(n, 1 - N_OUT, 2))
                for j in range(2):
                    three(Q_BANK, T * j, d, 2 * P * j, cq)
                for j in range(2):
                    before_last, last = three(QR_BANK, T * j, d, 2 * P * j + P, cq)
                before_last.then_inc(split_used, 1)
                last.then_inc(split_used, 1)

            def project_kv(p, n):
                wait(pe, kv_copied, value(p))
                d = (n.static + 1) % 2
                pe.wait_ge(lo_ready, value(n, 2 - N_OUT, 2))
                for j in range(2):
                    three(K_BANK, T * j, d, P * j, ckv)
                last = None
                for tt in range(2):
                    for kt in range(RT):
                        wa = slice(kt * 512 + 2 * P, kt * 512 + 4 * P)
                        for m, (wi, xi) in enumerate(((0, 0), (0, 1), (1, 0))):
                            before_last, last = last, pe.matmul(ps[:, V_BANK, T * tt:T * tt + T], ckv[:, kt, xi, P * tt:P * tt + P], wsp[:, d, wi, wa],
                                                                start=kt == 0 and m == 0, stop=kt == RT - 1 and m == 2)
                before_last.then_inc(split_used, 1)
                last.then_inc(split_used, 1)

            def score(p):
                pe.wait_ge(kv_copied, value(p, 1))
                pe.wait_ge(q_copied, value(p, 1))
                pe.wait_ge(q_ready, value(p, 1))
                wait(pe, masked, value(p))
                for j in range(2):
                    for t in range(2):
                        at, keys = (0, P) if t == 0 else (P, T)
                        pe.matmul(ps[:, SCORE_BANK + j, at:at + keys], qn[:, j, P * t:P * t + P], kn[:, j, 0:keys], start=True, stop=False)
                        last = pe.matmul(ps[:, SCORE_BANK + j, at:at + keys], qr[:, j, P * t:P * t + P], krope[:, 0:keys], start=False, stop=True)
                last.then_inc(scores, 1)

            def transpose(p):
                pe.wait_ge(probs_ready, value(p, 1))
                wait(pe, prt_ready, value(p))
                for j in range(2):
                    for k in range(3):
                        last = pe.transpose(ps[:, TURNED_BANK + j, P * k:P * k + P], pr[:, j, P * k:P * k + P], ident)
                last.then_inc(turned, 1)

            def attend(p, more):
                b = p.static % 2
                pe.wait_ge(prt_ready, value(p, 1))
                if more:
                    pe.wait_ge(q_copied, value(p, 2))
                for j in range(2):
                    pe.matmul(ps[:, out_bank(more), T * j:T * j + T], vv[:, b, 0, P * j:P * j + P], prt[:, j, 0:T], start=True, stop=False)
                    last = pe.matmul(ps[:, out_bank(more), T * j + P:T * j + T], vv[:, b, 1, P * j:P * j + P], prt[:, j, T:T + P], start=False, stop=True)
                last.then_inc(o_done, 1)

            pe.wait_ge(x_ready, 17)
            pe.wait_ge(summed, G_KR + 1)
            project_q(fixed(0), fixed(N_PAIR))
            sum_rank(S_CKV)
            keep_warm(K_BANK, 7)
            pe.wait_ge(x_ready, 18)
            project_kv(fixed(0), fixed(N_PAIR))

            def pair(p, n):
                score(p)
                project_q(ahead(p, 1), ahead(n, 2))
                transpose(p)
                project_kv(ahead(p, 1), ahead(n, 2))
                attend(p, True)
            looped(pe, 3, lambda i: [pair(at_loop(k, (2, i)), at_loop(N_PAIR + 2 * k, (4, i))) for k in range(2)])
            pair(fixed(6), fixed(N_PAIR + 12))
            score(fixed(7))
            pe.wait_ge(o_ready, 7)
            product(fixed(G_WO), fixed(N_WO), hid, None, 0, {1: lambda: transpose(fixed(7)), 2: lambda: attend(fixed(7), False),
                                                                  3: lambda: pe.wait_ge(o_ready, HEADS // 2)})
            for k in range(1, 4):
                product(fixed(G_WO + k), fixed(N_WO + GP * k), hid, None, 0, with_partials(fixed(G_WO + k), k))
            sum_y(S_Y2)
            sum_quarters(S_H3, sum_bank[S_Y2] + 1)
            mlp(pe, group, G_MLP1, N_MLP1, A_M1, 1, 0, 1, 16)
            sum_y(S_Y3)


def _tiles(w):
    k, n = w.shape
    return w.reshape(k // P, P, n // P, P).transpose(0, 2, 1, 3)


def _group(w, tiles):
    t = _tiles(w)[:, tiles]
    kt = t.shape[0]
    return t.reshape(kt // 4, 4, 4, P, P).transpose(0, 3, 1, 2, 4).reshape(kt // 4, P, PIECE)


def _streams(a):
    w = []

    def groups(m):
        for n in range(m.shape[1] // (GT * P)):
            w.append(_group(m, list(range(GT * n, GT * n + GT))))

    def mlp(l):
        for ch in range(CHUNKS):
            groups(a["mlp_w_up"][l][:, ch * D:(ch + 1) * D])
            groups(a["mlp_w_down"][l][ch * D:(ch + 1) * D])
    conv = [_group(a["conv_w_in"][0], [2 * g, 2 * g + 1, NT + 2 * g, NT + 2 * g + 1]) for g in range(IN_GROUPS)]
    w.append(np.stack(conv[:START_GROUPS], axis=1).reshape(-1, P, PIECE))
    w += conv[START_GROUPS:]
    groups(a["conv_w_out"][0])
    mlp(0)
    groups(a["w_dq"][0])
    kr = a["w_kr"]
    kr = np.concatenate([kr, kr[:, ROPE // 2:], kr[:, :ROPE // 2]], axis=1)
    w.append(kr.reshape(NT, P, P).transpose(1, 0, 2).reshape(1, P, PIECE))
    groups(a["w_dkv"])
    uk = a["w_uk"].reshape(RT, P, HEADS // 2, 2 * NOPE)
    uv = a["w_uv"].reshape(RT, P, HEADS // 2, 2 * VDIM)
    kv = np.concatenate([uk, uv], axis=3).transpose(2, 1, 0, 3).reshape(HEADS // 2, 1, P, PIECE)
    uq = a["w_uq"][0].reshape(RT, P, HEADS // 2, 2, NOPE + ROPE)
    half = NOPE + ROPE // 2
    uq = np.concatenate([uq, uq[..., half:], uq[..., NOPE:half]], axis=4)
    uq = uq.transpose(2, 1, 0, 3, 4).reshape(HEADS // 2, 1, P, PIECE)
    w.append(np.concatenate([uq, kv], axis=1).reshape(HEADS, P, PIECE))
    groups(a["w_o"][0])
    mlp(1)
    ada = [a["w_ada_mix"][0], a["w_ada_mlp"][0], a["w_ada_kv"], a["w_ada_mix"][1], a["w_ada_mlp"][1]]
    ada = np.concatenate([m.T.reshape(-1, P, D) for m in ada])
    first = [at + 4 * q + k for q in range(4) for at in (0, NT) for k in range(4)]
    ada = np.concatenate([ada[first], ada[A_START:]])
    return np.concatenate(w), ada


def _columns(a):
    def col(v):
        return np.asarray(v).reshape(-1, P).T
    bada = [a["b_ada_mix"][0], a["b_ada_mlp"][0], a["b_ada_kv"], a["b_ada_mix"][1], a["b_ada_mlp"][1]]
    b_in = a["conv_b_in"][0].reshape(2, IN_GROUPS, 2, P).transpose(1, 0, 2, 3).reshape(IN_GROUPS, GT, P)
    dw = np.concatenate([a["conv_dw"][0], a["conv_dw_b"][0][None]]).reshape(WIDTH + 1, IN_GROUPS, 2, P)
    conv = np.concatenate([b_in, dw.transpose(1, 2, 0, 3).reshape(IN_GROUPS, 2 * (WIDTH + 1), P)], axis=1)
    parts = [*bada, a["g_pre_mix"], a["g_post_mix"], a["g_pre_mlp"], a["g_post_mlp"], conv,
             a["conv_ln_g"], a["conv_ln_b"], a["conv_b_out"], a["g_kv"], a["g_ckv"], a["g_cq"]]
    return np.ascontiguousarray(np.concatenate([col(v) for v in parts], axis=1))


def _constants():
    k = np.zeros((P, K_ALL), np.float32)
    inv = 1.0 / (np.float32(THETA) ** (np.arange(0, ROPE, 2, dtype=np.float32) / np.float32(ROPE)))
    k[:, K_INV] = np.tile(inv.astype(np.float32), 4)
    k[:, K_SIGN] = np.where(np.arange(P) % ROPE < ROPE // 2, -1.0, 1.0)
    k[:, K_IDENT:K_IDENT + P] = np.eye(P)
    tri = np.where(np.arange(P)[None, :] <= np.arange(P)[:, None], 0.0, NEG)
    k[:, K_MASK:K_MASK + P] = tri
    k[:, K_MASK + 2 * P:] = tri
    return k


def kernel(**inputs):
    import concourse.bacc as _bacc
    from concourse.bass_utils import run_bass_kernel_spmd as _run

    a = {k: np.asarray(v) for k, v in inputs.items()}
    w, ada = _streams(a)
    arrays = {
        "x_t": np.ascontiguousarray(a["x"][0].T.reshape(NT, P, T).transpose(1, 0, 2)),
        "c": a["c"][0],
        "positions": a["positions"][0],
        "columns": _columns(a),
        "constants": _constants(),
        "w_stream": w,
        "ada_stream": ada,
    }
    nc = _bacc.Bacc("TRN2", target_bir_lowering=False, num_devices=1, dynamic_dma_scratch_size=1024)
    args = [nc.dram_tensor(n, v.shape, mybir.dt.from_np(v.dtype), kind="ExternalInput").ap() for n, v in arrays.items()]
    out = nc.dram_tensor("out_t", (P, NT, T), mybir.dt.float32, kind="ExternalOutput").ap()
    trunk(nc, *args, out)
    r = _run(nc, [arrays], core_ids=[0])
    got = r.results[0]["out_t"]
    return np.ascontiguousarray(np.asarray(got).transpose(1, 0, 2).reshape(D, T).T)[None]
```
